# Optimizing a Trainium2 kernel written in Bass

```python
import jax, jax.numpy as jnp
from jax import lax
import numpy as np

D_MODEL = 2048
BATCH = 1
SEQ = 256
DEPTH = 2

N_Q_HEADS = 16
N_KV_HEADS = 4
HEAD_DIM = 64
Q_PER_KV = N_Q_HEADS // N_KV_HEADS
ATTN_WIDTH = N_Q_HEADS * HEAD_DIM
KV_WIDTH = N_KV_HEADS * HEAD_DIM
WINDOW = 128
ROPE_THETA = 500000.0
ROPE_DIM = HEAD_DIM // 4
SGU_WIDTH = D_MODEL // 2
SGU_GROUPS = 8
SGU_GROUP_DIM = SGU_WIDTH // SGU_GROUPS
CHUNK = 128
D_FF = -(-8 * D_MODEL // (3 * 256)) * 256
OFF_Q = 0
OFF_K = OFF_Q + ATTN_WIDTH
OFF_V = OFF_K + KV_WIDTH
OFF_Z = OFF_V + KV_WIDTH
OFF_G = OFF_Z + 2 * SGU_WIDTH
IN_WIDTH = OFF_G + 2 * D_MODEL
EPS = 1e-5
NEG = -1e30

kernel_name = "hybrid_swa_sink_gmlp_gated_block"

def rmsnorm(x, g):
    xf = x.astype(jnp.float32)
    y = xf * lax.rsqrt(jnp.mean(xf * xf, axis=-1, keepdims=True) + EPS) * g.astype(jnp.float32)
    return y.astype(x.dtype)

def partial_rope(t, cos, sin):
    half = ROPE_DIM // 2
    t1 = t[..., :half].astype(jnp.float32)
    t2 = t[..., half:ROPE_DIM].astype(jnp.float32)
    rot = jnp.concatenate([t1 * cos - t2 * sin, t2 * cos + t1 * sin], axis=-1).astype(t.dtype)
    return jnp.concatenate([rot, t[..., ROPE_DIM:]], axis=-1)

def sliding_window_attention(q, k, v, sinks):
    B, S = q.shape[0], q.shape[1]
    nb = S // WINDOW
    qb = q.reshape(B, nb, WINDOW, N_KV_HEADS, Q_PER_KV, HEAD_DIM)

    def band(t):
        tb = t.reshape(B, nb, WINDOW, N_KV_HEADS, HEAD_DIM)
        prev = jnp.pad(tb, ((0, 0), (1, 0), (0, 0), (0, 0), (0, 0)))[:, :-1]
        return jnp.concatenate([prev, tb], axis=2)

    kb, vb = band(k), band(v)
    scores = jnp.einsum('bnqhgd,bnkhd->bnhgqk', qb, kb).astype(jnp.float32) * (HEAD_DIM ** -0.5)
    qi = jnp.arange(WINDOW)[:, None]
    kj = jnp.arange(2 * WINDOW)[None, :]
    rel = qi + WINDOW - kj
    band_ok = (rel >= 0) & (rel < WINDOW)
    blk_ok = (jnp.arange(nb)[:, None, None] > 0) | (kj >= WINDOW)[None]
    mask = band_ok[None] & blk_ok
    scores = jnp.where(mask[None, :, None, None], scores, NEG)
    sink = sinks.astype(jnp.float32).reshape(N_KV_HEADS, Q_PER_KV)[None, None, :, :, None, None]
    sink = jnp.broadcast_to(sink, scores.shape[:-1] + (1,))
    probs = jax.nn.softmax(jnp.concatenate([scores, sink], axis=-1), axis=-1)[..., :-1]
    out = jnp.einsum('bnhgqk,bnkhd->bnqhgd', probs.astype(v.dtype), vb)
    return out.reshape(B, S, ATTN_WIDTH)

def spatial_gating(z, ln_g, ln_b, w_s, b_s):
    B, S = z.shape[0], z.shape[1]
    u, v = jnp.split(z, 2, axis=-1)
    vf = v.astype(jnp.float32)
    mu = jnp.mean(vf, axis=-1, keepdims=True)
    var = jnp.mean(jnp.square(vf - mu), axis=-1, keepdims=True)
    vn = ((vf - mu) * lax.rsqrt(var + EPS) * ln_g.astype(jnp.float32) + ln_b.astype(jnp.float32)).astype(z.dtype)
    vc = vn.reshape(B, S // CHUNK, CHUNK, SGU_GROUPS, SGU_GROUP_DIM)
    causal = jnp.tril(jnp.ones((CHUNK, CHUNK), dtype=bool))
    w = jnp.where(causal[None], w_s, jnp.zeros_like(w_s))
    sv = jnp.einsum('gts,bnsgc->bntgc', w, vc) + b_s.T[None, None, :, :, None]
    return u * sv.reshape(B, S, SGU_WIDTH)

def setup_inputs(seed: int = 0) -> dict:
    key = jax.random.key(seed)
    ks = jax.random.split(key, 20)
    f32 = jnp.float32
    nrm = lambda k, shape, scale: jax.random.normal(k, shape, f32) * scale
    x = jax.random.normal(ks[0], (BATCH, SEQ, D_MODEL), f32)
    offset = jax.random.randint(ks[1], (BATCH, 1), 0, 4096, dtype=jnp.int32)
    positions = (jnp.arange(SEQ, dtype=jnp.int32)[None, :] + offset).astype(jnp.int32)
    return {
        "x": x,
        "positions": positions,
        "norm1_g": 1.0 + nrm(ks[2], (DEPTH, D_MODEL), 0.02),
        "w_in": nrm(ks[3], (DEPTH, D_MODEL, IN_WIDTH), D_MODEL ** -0.5),
        "b_in": nrm(ks[4], (DEPTH, IN_WIDTH), 0.02),
        "sinks": nrm(ks[5], (DEPTH, N_Q_HEADS), 1.0),
        "sgu_ln_g": 1.0 + nrm(ks[6], (DEPTH, SGU_WIDTH), 0.02),
        "sgu_ln_b": nrm(ks[7], (DEPTH, SGU_WIDTH), 0.02),
        "sgu_w": nrm(ks[8], (DEPTH, SGU_GROUPS, CHUNK, CHUNK), CHUNK ** -0.5),
        "sgu_b": 1.0 + nrm(ks[9], (DEPTH, SGU_GROUPS, CHUNK), 0.02),
        "w_attn_branch": nrm(ks[10], (DEPTH, ATTN_WIDTH, D_MODEL), ATTN_WIDTH ** -0.5),
        "w_sgu_branch": nrm(ks[11], (DEPTH, SGU_WIDTH, D_MODEL), SGU_WIDTH ** -0.5),
        "w_out": nrm(ks[12], (DEPTH, D_MODEL, D_MODEL), D_MODEL ** -0.5),
        "norm2_g": 1.0 + nrm(ks[13], (DEPTH, D_MODEL), 0.02),
        "w_gate_up": nrm(ks[14], (DEPTH, D_MODEL, 2 * D_FF), D_MODEL ** -0.5),
        "w_down": nrm(ks[15], (DEPTH, D_FF, D_MODEL), D_FF ** -0.5),
        "final_g": 1.0 + nrm(ks[16], (D_MODEL,), 0.02),
    }

def reference(x, positions, norm1_g, w_in, b_in, sinks, sgu_ln_g, sgu_ln_b, sgu_w, sgu_b,
              w_attn_branch, w_sgu_branch, w_out, norm2_g, w_gate_up, w_down, final_g):
    B, S = x.shape[0], x.shape[1]
    inv_freq = ROPE_THETA ** (-jnp.arange(0, ROPE_DIM, 2, dtype=jnp.float32) / ROPE_DIM)
    ang = positions.astype(jnp.float32)[..., None] * inv_freq
    cos = jnp.cos(ang)[:, :, None, :]
    sin = jnp.sin(ang)[:, :, None, :]
    h = x
    for l in range(DEPTH):
        xn = rmsnorm(h, norm1_g[l])
        proj = jnp.einsum('bsd,de->bse', xn, w_in[l]) + b_in[l]
        q = proj[..., OFF_Q:OFF_K].reshape(B, S, N_Q_HEADS, HEAD_DIM)
        k = proj[..., OFF_K:OFF_V].reshape(B, S, N_KV_HEADS, HEAD_DIM)
        v = proj[..., OFF_V:OFF_Z].reshape(B, S, N_KV_HEADS, HEAD_DIM)
        z = jax.nn.gelu(proj[..., OFF_Z:OFF_G], approximate=False)
        gates = jax.nn.sigmoid(proj[..., OFF_G:].astype(jnp.float32)).astype(h.dtype)
        g_attn, g_sgu = jnp.split(gates, 2, axis=-1)
        q = partial_rope(q, cos, sin)
        k = partial_rope(k, cos, sin)
        y_attn = sliding_window_attention(q, k, v, sinks[l])
        y_sgu = spatial_gating(z, sgu_ln_g[l], sgu_ln_b[l], sgu_w[l], sgu_b[l])
        merged = (g_attn * jnp.einsum('bse,ed->bsd', y_attn, w_attn_branch[l])
                  + g_sgu * jnp.einsum('bse,ed->bsd', y_sgu, w_sgu_branch[l]))
        h = h + jnp.einsum('bsd,de->bse', merged, w_out[l])
        hn = rmsnorm(h, norm2_g[l])
        gu = jnp.einsum('bsd,df->bsf', hn, w_gate_up[l])
        gate, up = jnp.split(gu, 2, axis=-1)
        h = h + jnp.einsum('bsf,fd->bsd', jax.nn.silu(gate) * up, w_down[l])
    return rmsnorm(h, final_g)


_drawn_inputs = setup_inputs


def setup_inputs(seed=0):
    import zlib

    import numpy as np

    out = dict(_drawn_inputs(seed))
    spreads = {}
    factors = {'norm1_g': 3.42,
     'sinks': 11.677,
     'sgu_ln_g': 8.0,
     'sgu_ln_b': 8.0,
     'sgu_b': 5.573,
     'norm2_g': 8.226,
     'final_g': 8.452,
     'b_in': 3.588}
    for name, (base, spread) in spreads.items():
        noise = np.random.default_rng([zlib.crc32(name.encode()), seed]).standard_normal(out[name].shape)
        drawn = base * np.exp(spread * noise) if base else spread * noise
        out[name] = __import__('jax').numpy.asarray(drawn.astype(out[name].dtype))
    for name, factor in factors.items():
        out[name] = (out[name] * factor).astype(out[name].dtype)
    return out
```

```python
import math
from contextlib import ExitStack

import numpy as np

import concourse.bass as bass
from concourse import mybir

F32 = mybir.dt.float32
F32R = mybir.dt.float32r
I32 = mybir.dt.int32
ACT = mybir.ActivationFunctionType
ALU = mybir.AluOpType
AX = mybir.AxisListType

P = 128
DEPTH = 2
D = 2048
SEQ = 256
TB = SEQ // P
HQ, HKV, DH = 16, 4, 64
GQ = HQ // HKV
ROPE = DH // 4
HALF = ROPE // 2
THETA = 500000.0
W_SGU = D // 2
GROUPS = 8
DFF = -(-8 * D // (3 * 256)) * 256
OFF_Q, OFF_K = 0, HQ * DH
OFF_Z = OFF_K + 2 * HKV * DH
OFF_G = OFF_Z + 2 * W_SGU
IN_W = OFF_G + 2 * D
EPS = 1e-5
NEG = -1e30

N = 512
KB_U = 2
KB = D // P
UNITS = KB // KB_U
SLOTS = 4
AHEAD = 3
NCH = D // N

FJ = 4
N_J = DFF // N
FULL_GROUPS = N_J // FJ
J_LAST = N_J - FULL_GROUPS * FJ
GRP_UNITS = FJ * 2 * UNITS + NCH * FJ * 4 // KB_U
DOWN_LAST = J_LAST * 4 // KB_U

U_Z = 0
U_QKV = U_Z + 4 * UNITS
U_G = U_QKV + 3 * UNITS
U_ATT = U_G + 8 * UNITS
U_SGU = U_ATT + NCH * UNITS // 2
U_WO = U_SGU + NCH * UNITS // 2
U_FF = U_WO + NCH * UNITS
U_LAST = U_FF + FULL_GROUPS * GRP_UNITS
NU = U_LAST + J_LAST * 2 * UNITS + NCH * DOWN_LAST

SET0 = dict(z=0, qkv=2, g=4, att=8, sgu=10, wo=12, ff=14)
SET1 = dict(z=0, qkv=2, g=3, att=7, sgu=9, wo=11, ff=13)
N_SET0 = SET0["ff"] + N_J + 2 * (FULL_GROUPS + 1)
N_SET1 = SET1["ff"] + N_J + 2 * (FULL_GROUPS + 1)

T0 = dict(sgu=0, y=2, m=6, h=10, a=14, x=14 + N_J)
T1 = dict(sgu=0, m=2, h=6, a=10, x=10 + N_J)
N_T0, N_T1 = T0["x"] + 4, T1["x"] + 4
N_PRE = 4
N_STR = 7
N_SP = 16
N_CP = 20
N_PV = 12
N_SAVE = 8
B_SET0, B_SET1 = 8, 7

TILES = [(0, 4, 0, P), (1, 2, 0, 2 * P), (1, 2, 2, 2 * P)]
S_AT, PT_AT, PV_AT, Y_AT = (1, 5, 9), (4, 8, 12), (5, 9, 13), 15

G_N1, G_FIN, G_N2 = 0, DEPTH * KB, (DEPTH + 1) * KB
G_SB = G_N2 + DEPTH * KB
G_ROWS = G_SB + DEPTH * GROUPS

TWO_PI = 2 * math.pi
PI_PARTS = []
_rest = TWO_PI
for _ in range(3):
    _scale = 2.0 ** (7 - math.floor(math.log2(_rest)))
    PI_PARTS.append(math.floor(_rest * _scale) / _scale)
    _rest -= PI_PARTS[-1]
PI_PARTS.append(_rest)
MAGIC = 1.5 * 2.0**23
PI_IN = 3.1415925


class Steps:

    def __init__(self, eng, sem, per_call):
        self.eng, self.sem, self.per_call = eng, sem, per_call

    def begin(self, call):
        self.base, self.k = call * self.per_call, 0

    def __call__(self, ins, wait=True):
        self.k += 1
        ins.then_inc(self.sem, 1)
        if wait:
            self.eng.wait_ge(self.sem, self.base + self.k)

    def end(self):
        assert self.k == self.per_call, (self.k, self.per_call)


def trunk(nc, x, positions, norm1_g, w_in, b_in, sinks, sgu_ln_g, sgu_ln_b, sgu_w, sgu_b,
          w_attn_branch, w_sgu_branch, w_out, norm2_g, w_gate_up, w_down, final_g, out):
    ctx = ExitStack()
    with ctx:
        at = [(nc.sbuf_base + 63) // 64 * 64]

        def sb(name, shape, dt=F32, offset=None):
            if offset is None:
                offset = at[0]
                at[0] += (math.prod(shape[1:]) * 4 + 31) // 32 * 32
                assert at[0] <= nc.sbuf_usable_end, name
            return nc.alloc_sbuf_tensor_at(name, shape, dt, offset=offset)

        def psum(name, shape):
            return ctx.enter_context(nc.psum_tensor(name, shape, F32))

        def sem(name):
            return ctx.enter_context(nc.semaphore(name))

        raw = sb("raw", [P, SLOTS, KB_U, N])
        w_hi = sb("w_hi", [P, SLOTS, KB_U, N], F32R)
        w_lo = sb("w_lo", [P, SLOTS, KB_U, N], F32R)
        a_hi = sb("a_hi", [P, KB, SEQ], F32R)
        a_lo = sb("a_lo", [P, KB, SEQ], F32R)
        b_at = at[0]
        b_hi = sb("b_hi", [P, KB, SEQ], F32R)
        b_lo = sb("b_lo", [P, KB, SEQ], F32R)
        c_at = at[0]
        c_hi = sb("c_hi", [P, KB, SEQ], F32R)
        c_lo = sb("c_lo", [P, KB, SEQ], F32R)
        fin_g = sb("fin_g", [P, D], F32, offset=b_at)
        gates = sb("gates", [P, TB, 2 * D], F32, offset=c_at)
        ln_gb = sb("ln_gb", [P, 2, W_SGU], F32, offset=c_at)
        ws = sb("ws", [P, GROUPS, P], F32, offset=c_at + 8 * W_SGU)
        ws_t = sb("ws_t", [P, GROUPS, P], F32, offset=c_at + 8 * W_SGU + 4 * GROUPS * P)
        v_sq = sb("v_sq", [P, TB, W_SGU], F32, offset=c_at + 8 * W_SGU + 8 * GROUPS * P)
        h = sb("h", [P, TB, D])
        z = sb("z", [P, TB, 2 * W_SGU])
        q_t = sb("q_t", [P, HQ // 2, SEQ])
        k_z = sb("k_z", [P, HKV, 2, SEQ])
        v_s = sb("v_s", [P, TB, HKV * DH])
        q_g = sb("q_g", [P, 2, SEQ])
        st = sb("st", [P, TB, N])
        gst = sb("gst", [P, TB, N])
        scores = sb("scores", [P, N])
        probs = sb("probs", [P, N])
        probs_t = sb("probs_t", [P, N])
        y_s = sb("y_s", [P, TB, GQ * DH])
        bias = sb("bias", [P, 2, N])
        ident = sb("ident", [P, P])
        mask0 = sb("mask0", [P, P])
        mask1 = sb("mask1", [P, 2 * P])
        grow = sb("grow", [P, P])
        gain = sb("gain", [P, G_ROWS])
        sink = sb("sink", [P, DEPTH * HQ])
        pos_i = sb("pos_i", [P, TB], I32)
        pos_f = sb("pos_f", [P, TB])
        freq = sb("freq", [P, HALF])
        ang = sb("ang", [P, TB, HALF])
        turns = sb("turns", [P, TB, HALF])
        sin_h = sb("sin_h", [P, TB, HALF])
        sin = sb("sin", [P, TB, HALF])
        cos = sb("cos", [P, TB, HALF])
        rot = sb("rot", [P, 4, TB * 8 * HALF])
        ss_x, ss_h = sb("ss_x", [P, TB]), sb("ss_h", [P, TB])
        rs_x, rs_h = sb("rs_x", [P, TB]), sb("rs_h", [P, TB])
        mhalf = sb("mhalf", [P, TB])
        v_sum, v_ss, v_nmu, v_rs = (sb(f"v{i}", [P, TB]) for i in range(4))
        mx, nmx, sd, es, den, dsum, rden = (sb(f"sm{i}", [P, GQ]) for i in range(7))

        acc = psum("acc", [P, 2, TB, N])
        tps = [psum(f"tps{b}", [P, N]) for b in range(2)]
        small = psum("small", [P, N])
        cps = psum("cps", [P, N])

        raw_landed = [sem(f"raw_landed{s}") for s in range(SLOTS)]
        bias_landed = [sem(f"bias_landed{s}") for s in range(2)]
        x_landed = [sem(f"x_landed{c}") for c in range(NCH)]
        rows_landed, sink_landed, pos_landed = sem("rows_landed"), sem("sink_landed"), sem("pos_landed")
        ln_landed, ws_landed, fin_landed, stored = sem("ln_landed"), sem("ws_landed"), sem("fin_landed"), sem("stored")
        hi_done = sem("hi_done")
        lo_done = sem("lo_done")
        unit_used = sem("unit_used")
        set_read = [sem(f"set_read{s}") for s in range(2)]
        st_ready = sem("st_ready")
        t_done = [sem(f"t_done{b}") for b in range(2)]
        t_hi = [sem(f"t_hi{b}") for b in range(2)]
        t_lo = [sem(f"t_lo{b}") for b in range(2)]
        small_done, small_read = sem("small_done"), sem("small_read")
        cp_done, cp_read = sem("cp_done"), sem("cp_read")
        pv_done, pv_read = sem("pv_done"), sem("pv_read")
        qg_ready = sem("qg_ready")
        soft = sem("soft")
        exp_done = sem("exp_done")
        den_step = sem("den_step")
        h_saved = sem("h_saved")
        ss_done = sem("ss_done")
        rs_step, rs_ready = sem("rs_step"), sem("rs_ready")
        gelu_v, gelu_u = sem("gelu_v"), sem("gelu_u")
        mu_ready, vss_done = sem("mu_ready"), sem("vss_done")
        lnr_step, lnr_ready = sem("lnr_step"), sem("lnr_ready")
        ln_step = sem("ln_step")
        sv_step, sgu_y = sem("sv_step"), sem("sgu_y")
        rope_step = sem("rope_step")
        m_step = sem("m_step")
        silu_done, sig_done = sem("silu_done"), sem("sig_done")
        ws_masked = sem("ws_masked")
        const_step, consts = sem("const_step"), sem("consts")
        trig, sin_done = sem("trig"), sem("sin_done")
        rows_done = sem("rows_done")
        fin_step = sem("fin_step")

        def not_negative(v):
            return nc.s_assert_within(v, 0, None, skip_runtime_bounds_check_because="j > 0 here")

        block = ctx.enter_context(nc.Block())
        pos = positions.rearrange("a (t p) -> p (a t)", p=P)
        x_d = x.rearrange("a (t p) d -> p (a t) d", p=P)
        out_d = out.rearrange("a (t p) d -> p (a t) d", p=P)

        @block.sync
        def _(sp):
            def dma(dst, src, done):
                return sp.dma_start(dst, src).then_inc(done, 16)

            def load_bias(s, k, l, col):
                prev = sp.snap(k + 1)
                sp.wait_ge(set_read[s], prev)
                dma(bias[:, s], b_in[bass.ds(l, 1), bass.ds(col, N)].broadcast_to([P, N]), bias_landed[s])

            def stream(n0, slot0, units, w, l, row0, col, with_bias=None):
                for u in range(units):
                    slot = (slot0 + u) % SLOTS
                    free = sp.snap(n0 + u + 1)
                    src = w[bass.ds(l, 1), bass.ds(row0 + u * KB_U * P, KB_U * P), bass.ds(col, N)]
                    sp.wait_ge(lo_done, free)
                    dma(raw[:, slot], src.rearrange("l (k p) n -> p (l k) n", p=P), raw_landed[slot])
                    if u == 3 and with_bias is not None:
                        with_bias()

            dma(grow[G_N1:G_FIN], norm1_g.rearrange("l (k p) -> (l k) p", p=P), rows_landed)
            dma(grow[G_FIN:G_N2], final_g.rearrange("(k p) -> k p", p=P), rows_landed)
            dma(grow[G_N2:G_SB], norm2_g.rearrange("l (k p) -> (l k) p", p=P), rows_landed)
            dma(grow[G_SB:G_ROWS], sgu_b.rearrange("l g t -> (l g) t"), rows_landed)
            for c in range(NCH):
                dma(h[:, :, c * N:(c + 1) * N], x_d[:, :, c * N:(c + 1) * N], x_landed[c])
            sp.dma_start(pos_i[:], pos, allow_slow_non_contiguous=True).then_inc(pos_landed, 16)
            dma(sink[:], sinks.rearrange("(a l) h -> a (l h)", a=1).broadcast_to([P, DEPTH * HQ]), sink_landed)

            with sp.Fori(0, DEPTH) as l:
                nl = sp.snap(l * NU)
                with sp.Fori(0, 2) as i:
                    for b in range(2):
                        col = i * (-2 * N) + (OFF_Z + (2 + b) * N)
                        stream(nl + U_Z + (2 * i + b) * UNITS, 0, UNITS, w_in, l, 0, col,
                               lambda: load_bias(b, l * (N_SET1 if b else N_SET0) + i, l, col))
                    with sp.If(i == 0):
                        first = sp.snap(nl + SLOTS + UNITS)
                        sp.wait_ge(unit_used, first)
                        dma(ln_gb[:, 0], sgu_ln_g[bass.ds(l, 1), :].broadcast_to([P, W_SGU]), ln_landed)
                        dma(ln_gb[:, 1], sgu_ln_b[bass.ds(l, 1), :].broadcast_to([P, W_SGU]), ln_landed)
                        dma(ws[:], sgu_w[bass.ds(l, 1)].rearrange("l g t s -> t (l g) s"), ws_landed)
                stream(nl + U_QKV, 0, UNITS, w_in, l, 0, OFF_K,
                       lambda: load_bias(0, l * N_SET0 + SET0["qkv"], l, OFF_K))

                with sp.Fori(0, 2) as i:
                    def bias_q():
                        with sp.If(i == 0):
                            load_bias(1, l * N_SET1 + SET1["qkv"], l, i * N + OFF_Q)
                        with sp.Else():
                            load_bias(0, l * N_SET0 + (SET0["qkv"] + 1), l, i * N + OFF_Q)
                    stream(nl + (U_QKV + UNITS) + i * UNITS, 0, UNITS, w_in, l, 0, i * N + OFF_Q, bias_q)

                with sp.Fori(0, NCH) as g:
                    for b in range(2):
                        at_set = l * N_SET1 + SET1["g"] if b else l * N_SET0 + SET0["g"]
                        col = g * N + (OFF_G + b * D)
                        stream(nl + U_G + (b * UNITS) + g * (2 * UNITS), 0, UNITS, w_in, l, 0, col,
                               lambda: load_bias(b, at_set + g, l, col))
                with sp.Fori(0, NCH) as c:
                    stream(nl + U_ATT + c * (UNITS // 2), 0, UNITS // 2, w_attn_branch, l, 0, c * N)
                with sp.Fori(0, NCH) as c:
                    stream(nl + U_SGU + c * (UNITS // 2), 0, UNITS // 2, w_sgu_branch, l, 0, c * N)
                with sp.Fori(0, NCH) as c:
                    stream(nl + U_WO + c * UNITS, 0, UNITS, w_out, l, 0, c * N)

                def ffn_group(n0, j0, n_j, units):
                    with sp.Fori(0, n_j) as j:
                        nj = sp.snap(n0 + j * (2 * UNITS))
                        stream(nj, 0, UNITS, w_gate_up, l, 0, j * N + j0 * N)
                        stream(nj + UNITS, 0, UNITS, w_gate_up, l, 0, j * N + j0 * N + DFF)
                    with sp.Fori(0, 2) as i:
                        nd = sp.snap(n0 + n_j * 2 * UNITS + i * (2 * units))
                        for b in range(2):
                            stream(nd + b * units, b * units, units, w_down, l, j0 * N, i * (2 * N) + b * N)

                with sp.Fori(0, FULL_GROUPS) as f:
                    ffn_group(nl + U_FF + f * GRP_UNITS, f * FJ, FJ, UNITS)
                ffn_group(nl + U_LAST, FULL_GROUPS * FJ, J_LAST, DOWN_LAST)

            sp.wait_ge(unit_used, DEPTH * NU + (SLOTS - NCH * DOWN_LAST))
            dma(fin_g[:], final_g.rearrange("(a n) -> a n", a=1).broadcast_to([P, D]), fin_landed)
            for tb in range(TB):
                sp.wait_ge(fin_step, tb + 1)
                dma(out_d[:, tb], h[:, tb], stored)
            sp.wait_ge(stored, 16 * TB)

        @block.gpsimd
        def _(pool):
            k = 0

            def step(ins):
                nonlocal k
                k += 1
                ins.then_inc(const_step, 1)
                pool.wait_ge(const_step, k)

            step(nc.gpsimd.memset(ident[:], 0.0))
            step(nc.gpsimd.affine_select(out=ident[:], in_=ident[:], compare_op=ALU.not_equal, fill=1.0,
                                         base=0, pattern=[[-1, P]], channel_multiplier=1))
            pool.sem_inc(consts, 1)
            step(nc.gpsimd.memset(mask0[:], 0.0))
            step(nc.gpsimd.memset(mask1[:], 0.0))
            step(nc.gpsimd.memset(mhalf[:], -0.5))
            step(nc.gpsimd.affine_select(out=mask0[:], in_=mask0[:], compare_op=ALU.is_ge, fill=NEG,
                                         base=0, pattern=[[-1, P]], channel_multiplier=1))
            step(nc.gpsimd.affine_select(out=mask1[:, P:], in_=mask1[:, P:], compare_op=ALU.is_ge, fill=NEG,
                                         base=0, pattern=[[-1, P]], channel_multiplier=1))
            step(nc.gpsimd.affine_select(out=mask1[:, :P], in_=mask1[:, :P], compare_op=ALU.is_gt, fill=NEG,
                                         base=0, pattern=[[1, P]], channel_multiplier=-1))
            step(nc.gpsimd.memset(k_z[:], 0.0))
            pool.sem_inc(consts, 1)

            def inv_sqrt(to, sums, n, step_sem, k, ready):
                nc.gpsimd.tensor_scalar(to[:], sums[:], 1.0 / n, EPS, ALU.mult, ALU.add).then_inc(step_sem, 1)
                pool.wait_ge(step_sem, k)
                nc.gpsimd.tensor_tensor(to[:], to[:], mhalf[:], ALU.pow).then_inc(ready, 1)

            for l in range(DEPTH):
                pool.wait_ge(ss_done, 2 * l + 1)
                inv_sqrt(rs_x, ss_x, D, rs_step, 2 * l + 1, rs_ready)
                pool.wait_ge(ws_landed, 16 * l + 16)
                nc.gpsimd.affine_select(out=ws[:], in_=ws[:], compare_op=ALU.is_ge, fill=0.0, base=0,
                                        pattern=[[0, GROUPS], [-1, P]], channel_multiplier=1).then_inc(ws_masked, 1)
                pool.wait_ge(vss_done, l + 1)
                inv_sqrt(v_rs, v_ss, W_SGU, lnr_step, l + 1, lnr_ready)
                pool.wait_ge(ss_done, 2 * l + 2)
                inv_sqrt(rs_h, ss_h, D, rs_step, 2 * l + 2, rs_ready)
            pool.wait_ge(ss_done, 2 * DEPTH + 1)
            inv_sqrt(rs_x, ss_x, D, rs_step, 2 * DEPTH + 1, rs_ready)

        @block.tensor
        def _(pe):
            def products(n0, slot0, units, hi, lo, kb0, s, k, ready=None):
                for u in range(units):
                    yield u
                    if u == 0:
                        pe.wait_ge(set_read[s], k + 1)
                    if ready is not None:
                        ready(u)
                    pe.wait_ge(lo_done, n0 + (u + SLOTS + 1))
                    slot = (slot0 + u) % SLOTS
                    for q in range(KB_U):
                        kb = KB_U * u + q
                        for tb in range(TB):
                            toks = slice(tb * P, (tb + 1) * P)
                            for part, (left, right) in enumerate(((hi, w_hi), (hi, w_lo), (lo, w_hi))):
                                mm = nc.tensor.matmul(acc[:, s, tb], left[:, kb0 + kb, toks], right[:, slot, q],
                                                      start=(kb == 0 and part == 0),
                                                      stop=(kb == units * KB_U - 1 and part == 2))
                    mm.then_inc(unit_used, 1)

            def operand(j0, j1):
                def ready(u):
                    pe.wait_ge(t_lo[u % 2], (j1 if u % 2 else j0) + (u // 2 + 2))
                return ready

            def t_pair(j0, j1, src):
                for b, j in ((0, j0), (1, j1)):
                    pe.wait_ge(t_lo[b], j + 1)
                    for q in range(2):
                        for tb in range(TB):
                            col = (2 * b + q) * P
                            mm = nc.tensor.transpose(tps[b][:, (q * TB + tb) * P:(q * TB + tb + 1) * P],
                                                     src[:, tb, col:col + P], ident[:])
                    mm.then_inc(t_done[b], 1)

            def copied(job, srcs):
                pe.wait_ge(cp_read, job + 1)
                for n, src in enumerate(srcs):
                    mm = nc.tensor.transpose(cps[:, n * P:(n + 1) * P], src, ident[:])
                mm.then_inc(cp_done, 1)

            pe.sem_inc(unit_used, SLOTS)
            pe.wait_ge(consts, 1)
            pe.wait_ge(rows_landed, 64)
            nc.tensor.transpose(small[:, 0:G_ROWS], grow[0:G_ROWS, :], ident[0:G_ROWS, 0:G_ROWS]).then_inc(rows_done, 1)
            for c in range(NCH - 1):
                pe.wait_ge(x_landed[c], 16)
                t_pair(c, c, h[:, :, c * N:(c + 1) * N])

            with pe.Fori(0, DEPTH) as l:
                nl = pe.snap(l * NU)
                s0, s1 = pe.snap(l * N_SET0), pe.snap(l * N_SET1)
                j0, j1 = pe.snap(l * N_T0 + N_PRE), pe.snap(l * N_T1 + N_PRE)
                cp, sm, pv = pe.snap(l * N_CP), pe.snap(l * N_SP), pe.snap(l * N_PV)

                with pe.Fori(0, 2) as i:
                    ni = nl + U_Z + i * (2 * UNITS)
                    for u in products(ni, 0, UNITS, a_hi, a_lo, 0, 0, s0 + i, operand(j0 - 4, j1 - 4)):
                        if u == 2:
                            with pe.If(i == 0):
                                pe.wait_ge(set_read[1], s1 + 1)
                                t_pair(j0 - 1, j1 - 1, st)
                    for u in products(ni + UNITS, 0, UNITS, a_hi, a_lo, 0, 1, s1 + i):
                        pass

                def gmlp(j):
                    hh, tb = divmod(j, 2)
                    pe.wait_ge(small_read, sm + (j + 1))
                    for g in range(4):
                        col = W_SGU + (4 * hh + g) * P
                        mm = nc.tensor.matmul(small[:, g * P:(g + 1) * P], ws_t[:, 4 * hh + g], z[:, tb, col:col + P],
                                              start=True, stop=True)
                    mm.then_inc(small_done, 1)

                def gmlp_t(j):
                    hh, tb = divmod(j, 2)
                    b, job = j % 2, (j1 if j % 2 else j0) + j // 2
                    pe.wait_ge(sgu_y, 4 * l + (j + 1))
                    pe.wait_ge(t_lo[b], job + 1)
                    for g in range(4):
                        col = (4 * hh + g) * P
                        mm = nc.tensor.transpose(tps[b][:, g * P:(g + 1) * P], z[:, tb, col:col + P], ident[:])
                    mm.then_inc(t_done[b], 1)

                for u in products(nl + U_QKV, 0, UNITS, a_hi, a_lo, 0, 0, s0 + 2):
                    if u in (2, 4):
                        if u == 2:
                            pe.wait_ge(ws_masked, l + 1)
                            pe.wait_ge(pv_read, pv + 1)
                        w = (u - 2) // 2
                        copied(cp + w, [ws[:, 4 * w + g] for g in range(4)])
                for u in products(nl + U_QKV + UNITS, 0, UNITS, a_hi, a_lo, 0, 1, s1 + 2):
                    if u in (2, 4):
                        w = (u - 2) // 2
                        pe.wait_ge(st_ready, N_STR * l + 1)
                        copied(cp + (2 + w), [st[:, tb, (2 * w + kb) * P:(2 * w + kb + 1) * P]
                                              for kb in range(2) for tb in range(TB)])
                    if u == 1:
                        pe.wait_ge(ln_step, 4 * l + 4)
                        pe.wait_ge(cp_read, cp + 3)
                    if u % 2 == 1:
                        gmlp(u // 2)
                        if u > 1:
                            gmlp_t(u // 2 - 1)
                for u in products(nl + U_QKV + 2 * UNITS, 0, UNITS, a_hi, a_lo, 0, 0, s0 + 3):
                    if u == 1:
                        gmlp_t(3)
                    if u in (2, 4):
                        w = (u - 2) // 2
                        pe.wait_ge(st_ready, N_STR * l + 2)
                        copied(cp + (4 + w), [st[:, tb, (2 * w + kb) * P:(2 * w + kb + 1) * P]
                                              for kb in range(2) for tb in range(TB)])
                for w in range(2):
                    pe.wait_ge(st_ready, N_STR * l + 3)
                    copied(cp + (6 + w), [st[:, tb, (2 * w + kb) * P:(2 * w + kb + 1) * P]
                                          for kb in range(2) for tb in range(TB)])

                def attention(p, g):
                    for t, (qb, heads, h0, keys) in enumerate(TILES):
                        tile = pv + g * 3 + t
                        if p == PT_AT[t]:
                            pe.wait_ge(exp_done, tile + 2)
                            pe.wait_ge(pv_read, tile + 1)
                            copied(cp + g * 3 + (8 + t), [probs[:, n * P:(n + 1) * P] for n in range(4)])
                        if p == PV_AT[t]:
                            pe.wait_ge(cp_read, cp + g * 3 + (8 + t + 2))
                            for a in range(heads):
                                for kb in range(keys // P):
                                    n = a * (keys // P) + kb
                                    mm = nc.tensor.matmul(cps[:, a * DH:(a + 1) * DH], probs_t[:, n * P:(n + 1) * P],
                                                          v_s[:, kb, bass.ds(g * DH, DH)],
                                                          start=(kb == 0), stop=(kb == keys // P - 1))
                            mm.then_inc(pv_done, 1)
                    for t, (qb, heads, h0, keys) in enumerate(TILES):
                        if p == S_AT[t]:
                            if t == 0:
                                pe.wait_ge(qg_ready, HKV * l + g + 1)
                            pe.wait_ge(small_read, sm + g * 3 + (4 + t + 1))
                            for a in range(heads):
                                hd = h0 + a
                                k_ap = k_z[:, bass.ds(g, 1), hd % 2, 0:keys].rearrange("p g k -> p (g k)")
                                mm = nc.tensor.matmul(small[:, a * keys:(a + 1) * keys],
                                                      q_g[:, hd // 2, qb * P:(qb + 1) * P], k_ap,
                                                      start=True, stop=True)
                            mm.then_inc(small_done, 1)
                    if p == Y_AT:
                        pe.wait_ge(pv_read, pv + g * 3 + 4)
                        pe.wait_ge(t_lo[0], j0 + T0["y"] + g + 1)
                        for q in range(2):
                            for tb in range(TB):
                                mm = nc.tensor.transpose(tps[0][:, (q * TB + tb) * P:(q * TB + tb + 1) * P],
                                                         y_s[:, tb, q * P:(q + 1) * P], ident[:])
                        mm.then_inc(t_done[0], 1)

                with pe.Fori(0, NCH) as g:
                    ng = nl + U_G + g * (2 * UNITS)
                    for u in products(ng, 0, UNITS, a_hi, a_lo, 0, 0, s0 + SET0["g"] + g):
                        attention(u, g)
                    for u in products(ng + UNITS, 0, UNITS, a_hi, a_lo, 0, 1, s1 + SET1["g"] + g):
                        attention(UNITS + u, g)

                with pe.Fori(0, 2) as i:
                    for b in range(2):
                        def ready(u):
                            pe.wait_ge(t_lo[0], j0 + (T0["y"] + u + 2))
                        for u in products(nl + U_ATT + (2 * i + b) * (UNITS // 2), 0, UNITS // 2, b_hi, b_lo, 0, b,
                                          (s1 + SET1["att"] if b else s0 + SET0["att"]) + i, ready):
                            pass
                with pe.Fori(0, 2) as i:
                    def ready(u):
                        if u == 0:
                            pe.wait_ge(t_lo[1], j1 + (T1["sgu"] + 1 + 2))
                    ni = nl + U_SGU + i * UNITS
                    for u in products(ni, 0, UNITS // 2, b_hi, b_lo, KB // 2, 0, s0 + SET0["sgu"] + i, ready):
                        if u == 2:
                            with pe.If(i == 1):
                                pe.wait_ge(st_ready, N_STR * l + (3 + 2))
                                t_pair(j0 + (T0["m"] + 1), j1 + (T1["m"] + 1), st)
                    for u in products(ni + UNITS // 2, 0, UNITS // 2, b_hi, b_lo, KB // 2, 1, s1 + SET1["sgu"] + i):
                        if u == 2:
                            pe.wait_ge(st_ready, N_STR * l + 2 * i + (3 + 1))
                            t_pair(j0 + T0["m"] + 2 * i, j1 + T1["m"] + 2 * i, st)
                with pe.Fori(0, 2) as i:
                    ni = nl + U_WO + i * (2 * UNITS)
                    for u in products(ni, 0, UNITS, a_hi, a_lo, 0, 0, s0 + SET0["wo"] + i,
                                      operand(j0 + T0["m"], j1 + T1["m"])):
                        if u == 2:
                            with pe.If(i == 0):
                                pe.wait_ge(st_ready, N_STR * l + (3 + 4))
                                t_pair(j0 + (T0["m"] + 3), j1 + (T1["m"] + 3), st)
                            with pe.Else():
                                pe.wait_ge(set_read[1], s1 + (SET1["wo"] + 2))
                                t_pair(j0 + (T0["h"] + 1), j1 + (T1["h"] + 1), st)
                    for u in products(ni + UNITS, 0, UNITS, a_hi, a_lo, 0, 1, s1 + SET1["wo"] + i):
                        if u == 2:
                            pe.wait_ge(set_read[0], s0 + i + (SET0["wo"] + 2))
                            t_pair(j0 + T0["h"] + 2 * i, j1 + T1["h"] + 2 * i, st)

                def ffn_group(n0, m0, d0, n_j, units, last, group):
                    f0, f1 = s0 + SET0["ff"] + d0, s1 + SET1["ff"] + d0
                    with pe.Fori(0, n_j) as j:
                        nj = n0 + j * (2 * UNITS)
                        for u in products(nj, 0, UNITS, b_hi, b_lo, 0, 0, f0 + j,
                                          operand(j0 + T0["h"], j1 + T1["h"])):
                            if u == 2:
                                if not last:
                                    with pe.If(group * FJ + j == 0):
                                        pe.wait_ge(set_read[1], s1 + (SET1["wo"] + 3))
                                        t_pair(j0 + (T0["h"] + 3), j1 + (T1["h"] + 3), st)
                                with pe.If(j != 0):
                                    pe.wait_ge(set_read[1], f1 + j + 1)
                                    t_pair(j0 + T0["a"] + m0 + j - 1, j1 + T1["a"] + m0 + j - 1, st)
                        for u in products(nj + UNITS, 0, UNITS, b_hi, b_lo, 0, 1, f1 + j):
                            pass
                    with pe.Fori(0, 2) as i:
                        nd = n0 + n_j * 2 * UNITS + i * (2 * units)
                        for u in products(nd, 0, units, c_hi, c_lo, 0, 0, f0 + n_j + i,
                                          operand(j0 + T0["a"] + m0, j1 + T1["a"] + m0)):
                            if u == 2:
                                with pe.If(i == 0):
                                    pe.wait_ge(set_read[1], f1 + (n_j + 1))
                                    t_pair(j0 + T0["a"] + m0 + (n_j - 1), j1 + T1["a"] + m0 + (n_j - 1), st)
                                if last:
                                    with pe.If(i == 1):
                                        pe.wait_ge(set_read[1], f1 + (n_j + 2))
                                        t_pair(j0 + (T0["x"] + 1), j1 + (T1["x"] + 1), st)
                        for u in products(nd + units, units, units, c_hi, c_lo, 0, 1, f1 + n_j + i):
                            if u == 2 and last:
                                pe.wait_ge(set_read[0], f0 + i + (n_j + 2))
                                t_pair(j0 + T0["x"] + 2 * i, j1 + T1["x"] + 2 * i, st)

                with pe.Fori(0, FULL_GROUPS) as f:
                    ffn_group(nl + U_FF + f * GRP_UNITS, f * FJ, f * (FJ + 2), FJ, UNITS, False, f)
                ffn_group(nl + U_LAST, FULL_GROUPS * FJ, FULL_GROUPS * (FJ + 2), J_LAST, DOWN_LAST, True, None)

        @block.scalar
        def _(act):
            def split_hi(n, slot):
                act.wait_ge(raw_landed[slot], (n - slot) * (16 // SLOTS) + 16)
                act.wait_ge(unit_used, n + 1)
                nc.scalar.activation(w_hi[:, slot], raw[:, slot], ACT.Copy).then_inc(hi_done, 1)

            def splitting(n0, slot0, units, stop=None):
                for u in range(units):
                    yield u
                    if stop is not None and u + AHEAD >= units:
                        with act.If(stop == 0):
                            split_hi(n0 + (u + AHEAD), (slot0 + u + AHEAD) % SLOTS)
                    else:
                        split_hi(n0 + (u + AHEAD), (slot0 + u + AHEAD) % SLOTS)

            def hi_pair(j0, j1, hi, kb0, g0=None):
                for b, j in ((0, j0), (1, j1)):
                    act.wait_ge(t_done[b], j + 1)
                    if g0 is None:
                        a = nc.scalar.activation(hi[:, bass.ds(kb0 + 2 * b, 2)],
                                                 tps[b].rearrange("p (k t) -> p k t", k=2), ACT.Copy)
                    else:
                        for q in range(2):
                            a = nc.scalar.activation(hi[:, bass.ds(kb0 + (2 * b + q), 1)],
                                                     tps[b][:, q * SEQ:(q + 1) * SEQ].unsqueeze(1), ACT.Copy,
                                                     scale=gain[:, bass.ds(g0 + (2 * b + q), 1)])
                    a.then_inc(t_hi[b], 1)

            def save_h(s, k, c):
                act.wait_ge(set_read[s], k + 2)
                nc.scalar.activation(h[:, :, bass.ds(c * N, N)], st[:], ACT.Copy).then_inc(h_saved, 1)

            def sum_squares(to, saved):
                act.wait_ge(h_saved, saved + 1)
                for tb in range(TB):
                    a = nc.scalar.activation(z[:, tb], h[:, tb], ACT.Square, accum_out=to[:, tb:tb + 1])
                a.then_inc(ss_done, 1)

            for s in (cp_read, exp_done, h_saved):
                act.sem_inc(s, 1)
            act.wait_ge(small_read, 1)
            for c in range(NCH - 1):
                hi_pair(c, c, a_hi, 4 * c, 4 * c)
            act.wait_ge(trig, 9)
            nc.scalar.activation(sin[:], ang[:], ACT.Sin).then_inc(sin_done, 1)
            nc.scalar.activation(sin_h[:], ang[:], ACT.Sin, scale=0.5).then_inc(sin_done, 1)
            act.wait_ge(x_landed[NCH - 1], 16)
            act.wait_ge(consts, 2)

            with act.Fori(0, DEPTH) as l:
                nl = act.snap(l * NU)
                s0, s1 = act.snap(l * N_SET0), act.snap(l * N_SET1)
                j0, j1 = act.snap(l * N_T0 + N_PRE), act.snap(l * N_T1 + N_PRE)
                cp = act.snap(l * N_CP)
                for u in range(AHEAD):
                    split_hi(nl + u, u)
                with act.Fori(0, 2) as i:
                    for u in splitting(nl + U_Z + i * (2 * UNITS), 0, UNITS):
                        if u == 2:
                            with act.If(i == 0):
                                hi_pair(j0 - 1, j1 - 1, a_hi, KB - 4, l * KB + (KB - 4))
                                sum_squares(ss_x, N_SAVE * l)
                    for u in splitting(nl + U_Z + i * (2 * UNITS) + UNITS, 0, UNITS):
                        pass

                def gelu_steps(u):
                    if u == 1:
                        act.wait_ge(set_read[1], s1 + 3)
                        for tb in range(TB):
                            nc.scalar.activation(z[:, tb, W_SGU:], z[:, tb, W_SGU:], ACT.Gelu,
                                                 accum_out=v_sum[:, tb:tb + 1]).then_inc(gelu_v, 1)
                    if u == 2:
                        for tb in range(TB):
                            nc.scalar.activation(z[:, tb, :W_SGU], z[:, tb, :W_SGU], ACT.Gelu).then_inc(gelu_u, 1)
                    if u == 3:
                        act.wait_ge(mu_ready, l + 1)
                        for tb in range(TB):
                            a = nc.scalar.activation(v_sq[:, tb], z[:, tb, W_SGU:], ACT.Square,
                                                     bias=v_nmu[:, tb:tb + 1], accum_out=v_ss[:, tb:tb + 1])
                        a.then_inc(vss_done, 1)

                def copied(job, to, src=None):
                    act.wait_ge(cp_done, job + 1)
                    nc.scalar.activation(to, cps[:] if src is None else src, ACT.Copy).then_inc(cp_read, 1)

                def gmlp_hi(j):
                    hh, tb = divmod(j, 2)
                    b, job = j % 2, (j1 if j % 2 else j0) + j // 2
                    act.wait_ge(t_done[b], job + 1)
                    nc.scalar.activation(b_hi[:, KB // 2 + 4 * hh:KB // 2 + 4 * hh + 4, tb * P:(tb + 1) * P],
                                         tps[b].rearrange("p (k t) -> p k t", k=4), ACT.Copy).then_inc(t_hi[b], 1)

                for u in splitting(nl + U_QKV, 0, UNITS):
                    gelu_steps(u)
                    if u in (2, 4):
                        w = (u - 2) // 2
                        copied(cp + w, ws_t[:, 4 * w:4 * w + 4], cps.rearrange("p (g t) -> p g t", g=4))
                for u in splitting(nl + U_QKV + UNITS, 0, UNITS):
                    if u in (2, 4):
                        w = (u - 2) // 2
                        act.wait_ge(cp_done, cp + (2 + w + 1))
                        src = cps.rearrange("p (k t) -> p k t", k=2)
                        nc.scalar.activation(k_z[0:DH, w:HKV:2, 0], src[0:DH], ACT.Copy)
                        nc.scalar.activation(k_z[DH:P, 1 - w:HKV:2, 1], src[DH:P], ACT.Copy).then_inc(cp_read, 1)
                    if u % 2 == 1 and u > 1:
                        gmlp_hi(u // 2 - 1)
                for u in splitting(nl + U_QKV + 2 * UNITS, 0, UNITS):
                    if u == 1:
                        gmlp_hi(3)
                    if u in (2, 4):
                        w = (u - 2) // 2
                        copied(cp + (4 + w), q_t[:, 2 * w:2 * w + 2].rearrange("p k t -> p (k t)"))
                for w in range(2):
                    copied(cp + (6 + w), q_t[:, 4 + 2 * w:6 + 2 * w].rearrange("p k t -> p (k t)"))

                def attention(p, g):
                    if p == 0:
                        act.wait_ge(small_done, l * N_SP + g * 3 + 4)
                        act.wait_ge(cp_read, cp + (8 + 1))
                        nc.scalar.activation(q_g[:], q_t[:, bass.ds(g * 2, 2)], ACT.Copy).then_inc(qg_ready, 1)
                    for t, (qb, heads, h0, keys) in enumerate(TILES):
                        if p == PT_AT[t]:
                            copied(cp + g * 3 + (8 + t), probs_t[:])
                    for t, (qb, heads, h0, keys) in enumerate(TILES):
                        if p == S_AT[t]:
                            act.wait_ge(soft, 4 * (l * N_PV) + g * 12 + 4 * (t + 1))
                            for a in range(heads):
                                nc.scalar.activation(probs[:, a * keys:(a + 1) * keys], scores[:, a * keys:(a + 1) * keys],
                                                     ACT.Exp, bias=nmx[:, a:a + 1], accum_out=den[:, a:a + 1])
                            nc.scalar.activation(es[:, 0:heads], sd[:, 0:heads], ACT.Exp).then_inc(exp_done, 1)
                    if p == Y_AT:
                        act.wait_ge(t_done[0], j0 + T0["y"] + g + 1)
                        nc.scalar.activation(b_hi[:, bass.ds(g * 2, 2)], tps[0].rearrange("p (k t) -> p k t", k=2),
                                             ACT.Copy).then_inc(t_hi[0], 1)

                with act.Fori(0, NCH) as g:
                    ng = nl + U_G + g * (2 * UNITS)
                    for u in splitting(ng, 0, UNITS):
                        attention(u, g)
                    for u in splitting(ng + UNITS, 0, UNITS):
                        attention(UNITS + u, g)

                with act.Fori(0, 2) as i:
                    for b in range(2):
                        for u in splitting(nl + U_ATT + (2 * i + b) * (UNITS // 2), 0, UNITS // 2):
                            if u in (1, 2):
                                if u == 1:
                                    act.wait_ge(set_read[1], s1 + (SET1["att"] + 1))
                                col = (u - 1) * D + i * (2 * N) + b * N
                                blk = gates[:, :, bass.ds(col, N)]
                                nc.scalar.activation(blk, blk, ACT.Sigmoid).then_inc(sig_done, 1)
                with act.Fori(0, 2) as i:
                    ni = nl + U_SGU + i * UNITS
                    for u in splitting(ni, 0, UNITS // 2):
                        if u == 2:
                            with act.If(i == 1):
                                hi_pair(j0 + (T0["m"] + 1), j1 + (T1["m"] + 1), a_hi, 4)
                    for u in splitting(ni + UNITS // 2, 0, UNITS // 2):
                        if u == 2:
                            hi_pair(j0 + T0["m"] + 2 * i, j1 + T1["m"] + 2 * i, a_hi, 8 * i)
                n2 = G_N2 + l * KB
                with act.Fori(0, 2) as i:
                    ni = nl + U_WO + i * (2 * UNITS)
                    for u in splitting(ni, 0, UNITS):
                        if u == 2:
                            with act.If(i == 0):
                                hi_pair(j0 + (T0["m"] + 3), j1 + (T1["m"] + 3), a_hi, KB - 4)
                            with act.Else():
                                save_h(1, s1 + SET1["wo"], 1)
                                hi_pair(j0 + (T0["h"] + 1), j1 + (T1["h"] + 1), b_hi, 4, n2 + 4)
                    for u in splitting(ni + UNITS, 0, UNITS):
                        if u == 2:
                            save_h(0, s0 + SET0["wo"] + i, 2 * i)
                            hi_pair(j0 + T0["h"] + 2 * i, j1 + T1["h"] + 2 * i, b_hi, 8 * i, n2 + 8 * i)

                def ffn_group(n0, m0, d0, n_j, units, last, group):
                    f0, f1 = s0 + SET0["ff"] + d0, s1 + SET1["ff"] + d0
                    with act.Fori(0, n_j) as j:
                        nj = n0 + j * (2 * UNITS)
                        for u in splitting(nj, 0, UNITS):
                            if u == 2:
                                if not last:
                                    with act.If(group * FJ + j == 0):
                                        save_h(1, s1 + (SET1["wo"] + 1), 3)
                                        hi_pair(j0 + (T0["h"] + 3), j1 + (T1["h"] + 3), b_hi, KB - 4, n2 + (KB - 4))
                                        sum_squares(ss_h, N_SAVE * l + 4)
                                with act.If(j != 0):
                                    hi_pair(j0 + T0["a"] + m0 + j - 1, j1 + T1["a"] + m0 + j - 1, c_hi,
                                            not_negative(4 * j - 4))
                        for u in splitting(nj + UNITS, 0, UNITS):
                            if u == 1:
                                act.wait_ge(set_read[0], f0 + j + 2)
                                nc.scalar.activation(gst[:], gst[:], ACT.Silu).then_inc(silu_done, 1)
                    with act.Fori(0, 2) as i:
                        nd = n0 + n_j * 2 * UNITS + i * (2 * units)
                        for u in splitting(nd, 0, units):
                            if u == 2:
                                with act.If(i == 0):
                                    hi_pair(j0 + T0["a"] + m0 + (n_j - 1), j1 + T1["a"] + m0 + (n_j - 1), c_hi,
                                            4 * (n_j - 1))
                                if last:
                                    with act.If(i == 1):
                                        save_h(1, f1 + n_j, 1)
                                        hi_pair(j0 + (T0["x"] + 1), j1 + (T1["x"] + 1), a_hi, 4, (l + 1) * KB + 4)
                        for u in splitting(nd + units, units, units, stop=i if last else None):
                            if u == 2 and last:
                                save_h(0, f0 + n_j + i, 2 * i)
                                hi_pair(j0 + T0["x"] + 2 * i, j1 + T1["x"] + 2 * i, a_hi, 8 * i, (l + 1) * KB + 8 * i)

                with act.Fori(0, FULL_GROUPS) as f:
                    ffn_group(nl + U_FF + f * GRP_UNITS, f * FJ, f * (FJ + 2), FJ, UNITS, False, f)
                ffn_group(nl + U_LAST, FULL_GROUPS * FJ, FULL_GROUPS * (FJ + 2), J_LAST, DOWN_LAST, True, None)
                save_h(1, s1 + (N_SET1 - 1), 3)
            sum_squares(ss_x, N_SAVE * DEPTH)

        @block.vector
        def _(dve):
            def split_lo(n, slot):
                dve.wait_ge(hi_done, n + 1)
                nc.vector.tensor_tensor(w_lo[:, slot], raw[:, slot], w_hi[:, slot].bitcast(F32),
                                        ALU.subtract).then_inc(lo_done, 1)

            def splitting(n0, slot0, units, stop=None):
                for u in range(units):
                    yield u
                    if stop is not None and u + AHEAD >= units:
                        with dve.If(stop == 0):
                            split_lo(n0 + (u + AHEAD), (slot0 + u + AHEAD) % SLOTS)
                    else:
                        split_lo(n0 + (u + AHEAD), (slot0 + u + AHEAD) % SLOTS)

            def lo_pair(j0, j1, hi, lo, kb0, g0=None):
                for b, j in ((0, j0), (1, j1)):
                    dve.wait_ge(t_hi[b], j + 1)
                    if g0 is None:
                        kbs = bass.ds(kb0 + 2 * b, 2)
                        v = nc.vector.tensor_tensor(lo[:, kbs], tps[b].rearrange("p (k t) -> p k t", k=2),
                                                    hi[:, kbs].bitcast(F32), ALU.subtract)
                    else:
                        for q in range(2):
                            kbs = bass.ds(kb0 + (2 * b + q), 1)
                            v = nc.vector.scalar_tensor_tensor(
                                out=lo[:, kbs], in0=tps[b][:, q * SEQ:(q + 1) * SEQ].unsqueeze(1),
                                scalar=gain[:, bass.ds(g0 + (2 * b + q), 1)], in1=hi[:, kbs].bitcast(F32),
                                op0=ALU.mult, op1=ALU.subtract)
                    v.then_inc(t_lo[b], 1)

            def evac_proj(s, used, k_bias, dst, done):
                dve.wait_ge(unit_used, used + SLOTS)
                dve.wait_ge(bias_landed[s], 16 * k_bias + 16)
                for tb in range(TB):
                    v = nc.vector.scalar_tensor_tensor(out=dst(tb), in0=acc[:, s, tb], scalar=rs_x[:, tb:tb + 1],
                                                       in1=bias[:, s], op0=ALU.mult, op1=ALU.add)
                v.then_inc(done, 1)

            def evac_residual(s, used, c, to_st, saved=None, j1=None):
                dve.wait_ge(unit_used, used + SLOTS)
                cols = bass.ds(c * N, N)
                if to_st:
                    dve.wait_ge(t_done[1], j1)
                    dve.wait_ge(h_saved, saved + 1)
                nc.vector.tensor_tensor(st[:] if to_st else h[:, :, cols], acc[:, s], h[:, :, cols],
                                        ALU.add).then_inc(set_read[s], 1)

            dve.sem_inc(lo_done, SLOTS)
            for s in (set_read[0], t_lo[0], t_lo[1], pv_read):
                dve.sem_inc(s, 1)
            dve.wait_ge(rows_done, 1)
            nc.vector.tensor_copy(gain[:], small[:, 0:G_ROWS]).then_inc(small_read, 1)
            dve.wait_ge(small_read, 1)
            for c in range(NCH - 1):
                lo_pair(c, c, a_hi, a_lo, 4 * c, 4 * c)
            dve.wait_ge(x_landed[NCH - 1], 16)
            nc.vector.tensor_copy(st[:], h[:, :, D - N:]).then_inc(set_read[1], 1)
            inv_freq = np.float32(THETA) ** (-np.arange(0, ROPE, 2, dtype=np.float32) / np.float32(ROPE))
            for f in range(HALF):
                v = nc.vector.memset(freq[:, f:f + 1], float(inv_freq[f]))
            dve.wait_ge(pos_landed, 16)
            trig_step = Steps(dve, trig, 11)
            trig_step.begin(0)
            trig_step(nc.vector.tensor_copy(pos_f[:], pos_i[:]))
            trig_step(nc.vector.tensor_tensor(ang[:], pos_f[:].unsqueeze(2).broadcast_to([P, TB, HALF]),
                                              freq[:].unsqueeze(1).broadcast_to([P, TB, HALF]), ALU.mult))
            trig_step(nc.vector.tensor_scalar(turns[:], ang[:], 1.0 / TWO_PI, MAGIC, ALU.mult, ALU.add))
            trig_step(nc.vector.tensor_scalar(turns[:], turns[:], MAGIC, None, ALU.subtract))
            for part in PI_PARTS:
                trig_step(nc.vector.scalar_tensor_tensor(out=ang[:], in0=turns[:], scalar=-part, in1=ang[:],
                                                         op0=ALU.mult, op1=ALU.add))
            trig_step(nc.vector.tensor_scalar(ang[:], ang[:], PI_IN, -PI_IN, ALU.min, ALU.max))
            dve.wait_ge(sin_done, 2)
            trig_step(nc.vector.tensor_tensor(cos[:], sin_h[:], sin_h[:], ALU.mult))
            trig_step(nc.vector.tensor_scalar(cos[:], cos[:], -2.0, 1.0, ALU.mult, ALU.add))
            dve.wait_ge(consts, 2)
            dve.wait_ge(sink_landed, 16)
            trig_step.end()

            rope_steps = Steps(dve, rope_step, 6)
            with dve.Fori(0, DEPTH) as l:
                nl = dve.snap(l * NU)
                s0, s1 = dve.snap(l * N_SET0), dve.snap(l * N_SET1)
                j0, j1 = dve.snap(l * N_T0 + N_PRE), dve.snap(l * N_T1 + N_PRE)
                cp, sm, pv = dve.snap(l * N_CP), dve.snap(l * N_SP), dve.snap(l * N_PV)
                bias0, bias1 = dve.snap(l * B_SET0), dve.snap(l * B_SET1)
                for u in range(AHEAD):
                    split_lo(nl + u, u)
                with dve.Fori(0, 2) as i:
                    ni = nl + U_Z + i * (2 * UNITS)
                    for u in splitting(ni, 0, UNITS):
                        if u == 0:
                            with dve.If(i == 1):
                                evac_proj(1, ni, bias1, lambda tb: z[:, tb, 3 * N:4 * N], set_read[1])
                        if u == 2:
                            with dve.If(i == 0):
                                lo_pair(j0 - 1, j1 - 1, a_hi, a_lo, KB - 4, l * KB + (KB - 4))
                    for u in splitting(ni + UNITS, 0, UNITS):
                        if u == 0:
                            dve.wait_ge(rs_ready, 2 * l + 1)
                            evac_proj(0, ni + UNITS, bias0 + i,
                                      lambda tb: z[:, tb, bass.ds(2 * N - i * (2 * N), N)], set_read[0])

                def rope(call, heads):
                    rope_steps.begin(call)
                    hd = st[:, :, 0:heads * DH].rearrange("p t (h d) -> p t h d", d=DH)
                    t1, t2 = hd[:, :, :, 0:HALF], hd[:, :, :, HALF:ROPE]
                    c_, s_ = (a[:].unsqueeze(2).broadcast_to([P, TB, heads, HALF]) for a in (cos, sin))
                    tmp = [rot[:, n, 0:TB * heads * HALF].rearrange("p (t h d) -> p t h d", t=TB, h=heads)
                           for n in range(4)]
                    for n, (t, f) in enumerate(((t1, c_), (t2, s_), (t2, c_), (t1, s_))):
                        rope_steps(nc.vector.tensor_tensor(tmp[n], t, f, ALU.mult), wait=(n == 3))
                    rope_steps(nc.vector.tensor_tensor(t1, tmp[0], tmp[1], ALU.subtract), wait=False)
                    rope_steps(nc.vector.tensor_tensor(t2, tmp[2], tmp[3], ALU.add))
                    rope_steps.end()

                def layer_norm(u):
                    if u == 3:
                        dve.wait_ge(gelu_v, 2 * l + 2)
                        nc.vector.tensor_scalar(v_nmu[:], v_sum[:], -1.0 / W_SGU, None, ALU.mult).then_inc(mu_ready, 1)
                    if u in (5, 6):
                        tb = u - 5
                        if tb == 0:
                            dve.wait_ge(ln_landed, 32 * l + 32)
                            dve.wait_ge(lnr_ready, l + 1)
                            dve.wait_ge(mu_ready, l + 1)
                        v = z[:, tb, W_SGU:]
                        nc.vector.scalar_tensor_tensor(out=v, in0=v, scalar=v_nmu[:, tb:tb + 1], in1=ln_gb[:, 0],
                                                       op0=ALU.add, op1=ALU.mult).then_inc(ln_step, 1)
                    if u == 7:
                        dve.wait_ge(ln_step, 4 * l + 2)
                        for tb in range(TB):
                            v = z[:, tb, W_SGU:]
                            nc.vector.scalar_tensor_tensor(out=v, in0=v, scalar=v_rs[:, tb:tb + 1], in1=ln_gb[:, 1],
                                                           op0=ALU.mult, op1=ALU.add).then_inc(ln_step, 1)

                def gmlp(j):
                    hh, tb = divmod(j, 2)
                    dve.wait_ge(small_done, sm + (j + 1))
                    v = z[:, tb, W_SGU + hh * N:W_SGU + (hh + 1) * N].rearrange("p (g c) -> p g c", g=4)
                    sb_col = gain[:, bass.ds(G_SB + 4 * hh + l * GROUPS, 4)].unsqueeze(2).broadcast_to([P, 4, P])
                    nc.vector.tensor_tensor(v, small.rearrange("p (g c) -> p g c", g=4), sb_col,
                                            ALU.add).then_inc(small_read, 1)
                    dve.wait_ge(small_read, sm + (j + 2))
                    dve.wait_ge(gelu_u, 2 * l + 2)
                    uu = z[:, tb, hh * N:(hh + 1) * N]
                    nc.vector.tensor_tensor(uu, uu, z[:, tb, W_SGU + hh * N:W_SGU + (hh + 1) * N],
                                            ALU.mult).then_inc(sgu_y, 1)

                def gmlp_lo(j):
                    hh, tb = divmod(j, 2)
                    b, job = j % 2, (j1 if j % 2 else j0) + j // 2
                    dve.wait_ge(t_hi[b], job + 1)
                    to = (slice(None), slice(KB // 2 + 4 * hh, KB // 2 + 4 * hh + 4), slice(tb * P, (tb + 1) * P))
                    nc.vector.tensor_tensor(b_lo[to], tps[b].rearrange("p (k t) -> p k t", k=4),
                                            b_hi[to].bitcast(F32), ALU.subtract).then_inc(t_lo[b], 1)

                for u in splitting(nl + U_QKV, 0, UNITS):
                    if u == 0:
                        evac_proj(1, nl + U_QKV, bias1 + 1, lambda tb: z[:, tb, N:2 * N], set_read[1])
                    layer_norm(u)
                for u in splitting(nl + U_QKV + UNITS, 0, UNITS):
                    if u == 0:
                        dve.wait_ge(unit_used, nl + (U_QKV + UNITS + SLOTS))
                        dve.wait_ge(bias_landed[0], 16 * bias0 + 16 * 3)
                        dve.wait_ge(t_done[1], j1)
                        dve.wait_ge(h_saved, N_SAVE * l + 1)
                        dve.wait_ge(pv_done, pv)
                        kw = HKV * DH
                        for to, cols in ((st, slice(0, kw)), (v_s, slice(kw, 2 * kw))):
                            for tb in range(TB):
                                v = nc.vector.scalar_tensor_tensor(
                                    out=to[:, tb, 0:kw], in0=acc[:, 0, tb, cols], scalar=rs_x[:, tb:tb + 1],
                                    in1=bias[:, 0, cols], op0=ALU.mult, op1=ALU.add)
                        v.then_inc(set_read[0], 1)
                        dve.wait_ge(set_read[0], s0 + 4)
                        rope(3 * l, HKV)
                        kh = st[:].rearrange("p t (w k e d) -> p w t k e d", w=2, k=2, e=2)
                        for e in range(2):
                            v = nc.vector.tensor_copy(kh[:, 1, :, :, e], kh[:, 0, :, :, 1 - e])
                        v.then_inc(st_ready, 1)
                    if u % 2 == 1:
                        gmlp(u // 2)
                        if u > 1:
                            gmlp_lo(u // 2 - 1)

                def evac_q(s, used, k_bias, copied_jobs, call, k):
                    dve.wait_ge(cp_done, copied_jobs)
                    evac_proj(s, used, k_bias, lambda tb: st[:, tb], set_read[s])
                    dve.wait_ge(set_read[s], k + 2)
                    rope(call, 8)
                    dve.sem_inc(st_ready, 1)

                for u in splitting(nl + U_QKV + 2 * UNITS, 0, UNITS):
                    if u == 0:
                        evac_q(1, nl + (U_QKV + 2 * UNITS), bias1 + 2, cp + 4, 3 * l + 1, s1 + 2)
                    if u == 1:
                        gmlp_lo(3)
                evac_q(0, nl + U_G, bias0 + 3, cp + 6, 3 * l + 2, s0 + 3)

                def attention(p, g):
                    for t, (qb, heads, h0, keys) in enumerate(TILES):
                        tile = pv + g * 3 + t
                        if p == PT_AT[t]:
                            dve.wait_ge(exp_done, tile + 2)
                            nc.vector.tensor_tensor(dsum[:, 0:heads], den[:, 0:heads], es[:, 0:heads],
                                                    ALU.add).then_inc(den_step, 1)
                            dve.wait_ge(den_step, 2 * pv + 6 * g + (2 * t + 1))
                            nc.vector.reciprocal(rden[:, 0:heads], dsum[:, 0:heads]).then_inc(den_step, 1)
                        if p == PV_AT[t]:
                            dve.wait_ge(pv_done, tile + 1)
                            dve.wait_ge(den_step, 2 * pv + 6 * g + (2 * t + 2))
                            if t == 0:
                                dve.wait_ge(t_done[0], j0 + T0["y"] + g)
                            y = y_s[:, qb, h0 * DH:(h0 + heads) * DH].rearrange("p (h d) -> p h d", d=DH)
                            o = cps[:, 0:heads * DH].rearrange("p (h d) -> p h d", d=DH)
                            nc.vector.tensor_tensor(y, o, rden[:, 0:heads].unsqueeze(2).broadcast_to([P, heads, DH]),
                                                    ALU.mult).then_inc(pv_read, 1)
                    for t, (qb, heads, h0, keys) in enumerate(TILES):
                        tile = pv + g * 3 + t
                        if p == S_AT[t]:
                            job = sm + g * 3 + (4 + t)
                            dve.wait_ge(small_done, job + 1)
                            dve.wait_ge(exp_done, tile + 1)
                            mask = mask0 if qb == 0 else mask1
                            sc = scores[:].rearrange("p (h k) -> p h k", h=heads)
                            nc.vector.scalar_tensor_tensor(
                                out=sc, in0=small.rearrange("p (h k) -> p h k", h=heads), scalar=DH**-0.5,
                                in1=mask[:].unsqueeze(1).broadcast_to([P, heads, keys]),
                                op0=ALU.mult, op1=ALU.add).then_inc(small_read, 1)
                            dve.wait_ge(small_read, job + 2)
                            soft0 = 4 * pv + 12 * g + 4 * t
                            m = mx[:, 0:heads]
                            snk = sink[:, bass.ds(h0 + g * GQ + l * HQ, heads)]
                            nc.vector.tensor_reduce(m, sc, AX.X, ALU.max).then_inc(soft, 1)
                            dve.wait_ge(soft, soft0 + 1)
                            nc.vector.tensor_tensor(m, m, snk, ALU.max).then_inc(soft, 1)
                            dve.wait_ge(soft, soft0 + 2)
                            nc.vector.tensor_scalar(nmx[:, 0:heads], m, -1.0, None, ALU.mult).then_inc(soft, 1)
                            nc.vector.tensor_tensor(sd[:, 0:heads], snk, m, ALU.subtract).then_inc(soft, 1)
                    if p == Y_AT:
                        dve.wait_ge(t_hi[0], j0 + T0["y"] + g + 1)
                        kbs = bass.ds(g * 2, 2)
                        nc.vector.tensor_tensor(b_lo[:, kbs], tps[0].rearrange("p (k t) -> p k t", k=2),
                                                b_hi[:, kbs].bitcast(F32), ALU.subtract).then_inc(t_lo[0], 1)

                with dve.Fori(0, NCH) as g:
                    ng = nl + U_G + g * (2 * UNITS)
                    for u in splitting(ng, 0, UNITS):
                        if u == 0:
                            with dve.If(g != 0):
                                evac_proj(1, ng, bias1 + g + 2, lambda tb: gates[:, tb, bass.ds(D - N + g * N, N)],
                                          set_read[1])
                        attention(u, g)
                    for u in splitting(ng + UNITS, 0, UNITS):
                        if u == 0:
                            evac_proj(0, ng + UNITS, bias0 + g + 4, lambda tb: gates[:, tb, bass.ds(g * N, N)],
                                      set_read[0])
                        attention(UNITS + u, g)

                def gate_attn(s, used, c, sig):
                    dve.wait_ge(unit_used, used + SLOTS)
                    dve.wait_ge(sig_done, sig)
                    blk = gates[:, :, bass.ds(c * N, N)]
                    nc.vector.tensor_tensor(blk, acc[:, s], blk, ALU.mult).then_inc(set_read[s], 1)

                def merge(s, used, c, k):
                    dve.wait_ge(unit_used, used + SLOTS)
                    dve.wait_ge(t_done[1], j1 + T1["m"] + c)
                    dve.wait_ge(cp_done, cp + 8)
                    dve.wait_ge(sig_done, 8 * l + 8)
                    nc.vector.tensor_tensor(st[:], acc[:, s], gates[:, :, bass.ds(c * N + D, N)],
                                            ALU.mult).then_inc(set_read[s], 1)
                    dve.wait_ge(set_read[s], k + 2)
                    nc.vector.tensor_tensor(st[:], st[:], gates[:, :, bass.ds(c * N, N)], ALU.add).then_inc(st_ready, 1)

                hu = UNITS // 2
                with dve.Fori(0, 2) as i:
                    ni = nl + U_ATT + i * UNITS
                    for u in splitting(ni, 0, hu):
                        if u == 0:
                            with dve.If(i == 0):
                                evac_proj(1, ni, bias1 + (B_SET1 - 1), lambda tb: gates[:, tb, 2 * D - N:], set_read[1])
                            with dve.Else():
                                gate_attn(1, ni, 1, 8 * l + 4)
                    for u in splitting(ni + hu, 0, hu):
                        if u == 0:
                            gate_attn(0, ni + hu, 2 * i, 8 * l + 4 * i + 2)
                with dve.Fori(0, 2) as i:
                    ni = nl + U_SGU + i * UNITS
                    for u in splitting(ni, 0, hu):
                        if u == 0:
                            with dve.If(i == 0):
                                gate_attn(1, ni, 3, 8 * l + 8)
                            with dve.Else():
                                merge(1, ni, 1, s1 + SET1["sgu"])
                        if u == 2:
                            with dve.If(i == 1):
                                lo_pair(j0 + (T0["m"] + 1), j1 + (T1["m"] + 1), a_hi, a_lo, 4)
                    for u in splitting(ni + hu, 0, hu):
                        if u == 0:
                            merge(0, ni + hu, 2 * i, s0 + SET0["sgu"] + i)
                        if u == 2:
                            lo_pair(j0 + T0["m"] + 2 * i, j1 + T1["m"] + 2 * i, a_hi, a_lo, 8 * i)
                n2 = G_N2 + l * KB
                with dve.Fori(0, 2) as i:
                    ni = nl + U_WO + i * (2 * UNITS)
                    for u in splitting(ni, 0, UNITS):
                        if u == 0:
                            with dve.If(i == 0):
                                merge(1, ni, 3, s1 + (SET1["sgu"] + 1))
                            with dve.Else():
                                evac_residual(1, ni, 1, True, N_SAVE * l + 1, j1 + (T1["h"] + 1))
                        if u == 2:
                            with dve.If(i == 0):
                                lo_pair(j0 + (T0["m"] + 3), j1 + (T1["m"] + 3), a_hi, a_lo, KB - 4)
                            with dve.Else():
                                lo_pair(j0 + (T0["h"] + 1), j1 + (T1["h"] + 1), b_hi, b_lo, 4, n2 + 4)
                    for u in splitting(ni + UNITS, 0, UNITS):
                        if u == 0:
                            evac_residual(0, ni + UNITS, 2 * i, True, N_SAVE * l + 2 * i, j1 + T1["h"] + 2 * i)
                        if u == 2:
                            lo_pair(j0 + T0["h"] + 2 * i, j1 + T1["h"] + 2 * i, b_hi, b_lo, 8 * i, n2 + 8 * i)

                def swiglu(used, k_silu, j1_free, saved):
                    dve.wait_ge(unit_used, used + SLOTS)
                    dve.wait_ge(silu_done, k_silu)
                    dve.wait_ge(t_done[1], j1_free)
                    dve.wait_ge(h_saved, saved + 1)
                    for tb in range(TB):
                        v = nc.vector.scalar_tensor_tensor(out=st[:, tb], in0=acc[:, 1, tb], scalar=rs_h[:, tb:tb + 1],
                                                           in1=gst[:, tb], op0=ALU.mult, op1=ALU.mult)
                    v.then_inc(set_read[1], 1)

                def ffn_group(n0, m0, d0, n_j, units, last, group):
                    a0, a1 = j0 + T0["a"] + m0, j1 + T1["a"] + m0
                    silu0 = N_J * l + m0
                    saved = N_SAVE * l + 4
                    with dve.Fori(0, n_j) as j:
                        nj = n0 + j * (2 * UNITS)
                        for u in splitting(nj, 0, UNITS):
                            if u == 0:
                                if last:
                                    with dve.If(j == 0):
                                        evac_residual(1, nj, 3, False)
                                else:
                                    with dve.If(group * FJ + j == 0):
                                        evac_residual(1, nj, 3, True, N_SAVE * l + 3, j1 + (T1["h"] + 3))
                                    with dve.If(group * 2 * FJ + j == 2 * FJ):
                                        evac_residual(1, nj, 3, False)
                                with dve.If(j != 0):
                                    swiglu(nj, silu0 + j, a1 + j - 1, saved)
                            if u == 2:
                                if not last:
                                    with dve.If(group * FJ + j == 0):
                                        lo_pair(j0 + (T0["h"] + 3), j1 + (T1["h"] + 3), b_hi, b_lo, KB - 4,
                                                n2 + (KB - 4))
                                with dve.If(j != 0):
                                    lo_pair(a0 + j - 1, a1 + j - 1, c_hi, c_lo, not_negative(4 * j - 4))
                        for u in splitting(nj + UNITS, 0, UNITS):
                            if u == 0:
                                dve.wait_ge(unit_used, nj + (UNITS + SLOTS))
                                dve.wait_ge(rs_ready, 2 * l + 2)
                                for tb in range(TB):
                                    v = nc.vector.tensor_scalar(gst[:, tb], acc[:, 0, tb], rs_h[:, tb:tb + 1], None,
                                                                ALU.mult)
                                v.then_inc(set_read[0], 1)
                    with dve.Fori(0, 2) as i:
                        nd = n0 + n_j * 2 * UNITS + i * (2 * units)
                        for u in splitting(nd, 0, units):
                            if u == 0:
                                with dve.If(i == 0):
                                    swiglu(nd, silu0 + n_j, a1 + (n_j - 1), saved)
                                with dve.Else():
                                    evac_residual(1, nd, 1, last, saved + 1, j1 + (T1["x"] + 1))
                            if u == 2:
                                with dve.If(i == 0):
                                    lo_pair(a0 + (n_j - 1), a1 + (n_j - 1), c_hi, c_lo, 4 * (n_j - 1))
                                if last:
                                    with dve.If(i == 1):
                                        lo_pair(j0 + (T0["x"] + 1), j1 + (T1["x"] + 1), a_hi, a_lo, 4,
                                                (l + 1) * KB + 4)
                        for u in splitting(nd + units, units, units, stop=i if last else None):
                            if u == 0:
                                evac_residual(0, nd + units, 2 * i, last, saved + 2 * i, j1 + T1["x"] + 2 * i)
                            if u == 2 and last:
                                lo_pair(j0 + T0["x"] + 2 * i, j1 + T1["x"] + 2 * i, a_hi, a_lo, 8 * i,
                                        (l + 1) * KB + 8 * i)

                with dve.Fori(0, FULL_GROUPS) as f:
                    ffn_group(nl + U_FF + f * GRP_UNITS, f * FJ, f * (FJ + 2), FJ, UNITS, False, f)
                ffn_group(nl + U_LAST, FULL_GROUPS * FJ, FULL_GROUPS * (FJ + 2), J_LAST, DOWN_LAST, True, None)
                evac_residual(1, nl + NU, 3, True, N_SAVE * l + 7, j1 + (T1["x"] + 3))

            dve.wait_ge(rs_ready, 2 * DEPTH + 1)
            dve.wait_ge(fin_landed, 16)
            for tb in range(TB):
                nc.vector.scalar_tensor_tensor(out=h[:, tb], in0=h[:, tb], scalar=rs_x[:, tb:tb + 1], in1=fin_g[:],
                                               op0=ALU.mult, op1=ALU.mult).then_inc(fin_step, 1)


_INS = ["x", "positions", "norm1_g", "w_in", "b_in", "sinks", "sgu_ln_g", "sgu_ln_b", "sgu_w", "sgu_b",
        "w_attn_branch", "w_sgu_branch", "w_out", "norm2_g", "w_gate_up", "w_down", "final_g"]
_OUTS = [((1, SEQ, D), "float32")]


def kernel(**inputs):
    import numpy as _np
    import concourse.bacc as _bacc
    from concourse import mybir as _mybir
    from concourse.bass_utils import run_bass_kernel_spmd as _run

    nc = _bacc.Bacc("TRN2", target_bir_lowering=False, num_devices=1, dynamic_dma_scratch_size=1024)
    arrays, args = {}, []
    for name in _INS:
        a = _np.ascontiguousarray(inputs[name])
        arrays[f"in_{name}_dram"] = a
        args.append(nc.dram_tensor(f"in_{name}_dram", a.shape, _mybir.dt.from_np(a.dtype), kind="ExternalInput").ap())
    for i, (shape, dtype) in enumerate(_OUTS):
        dt = _mybir.dt.from_np(_np.dtype(dtype))
        args.append(nc.dram_tensor(f"out_{i}_dram", shape, dt, kind="ExternalOutput").ap())
    trunk(nc, *args)
    r = _run(nc, [arrays], core_ids=[0])
    got = tuple(r.results[0][f"out_{i}_dram"] for i in range(len(_OUTS)))
    return got[0]
```

```python
import math
from contextlib import ExitStack

import numpy as np

import concourse.bass as bass
from concourse import mybir

F32 = mybir.dt.float32
F32R = mybir.dt.float32r
I32 = mybir.dt.int32
ACT = mybir.ActivationFunctionType
ALU = mybir.AluOpType
AX = mybir.AxisListType

P = 128
DEPTH = 2
D = 2048
SEQ = 256
TB = SEQ // P
HQ, HKV, DH = 16, 4, 64
GQ = HQ // HKV
ROPE = DH // 4
HALF = ROPE // 2
THETA = 500000.0
W_SGU = D // 2
GROUPS = 8
DFF = -(-8 * D // (3 * 256)) * 256
OFF_Q, OFF_K = 0, HQ * DH
OFF_Z = OFF_K + 2 * HKV * DH
OFF_G = OFF_Z + 2 * W_SGU
IN_W = OFF_G + 2 * D
EPS = 1e-5
NEG = -1e30

N = 512
KB_U = 2
KB = D // P
UNITS = KB // KB_U
SLOTS = 4
AHEAD = 3
NCH = D // N

FJ = 4
N_J = DFF // N
FULL_GROUPS = N_J // FJ
J_LAST = N_J - FULL_GROUPS * FJ
GRP_UNITS = FJ * 2 * UNITS + NCH * FJ * 4 // KB_U
DOWN_LAST = J_LAST * 4 // KB_U

U_Z = 0
U_QKV = U_Z + 4 * UNITS
U_G = U_QKV + 3 * UNITS
U_ATT = U_G + 8 * UNITS
U_SGU = U_ATT + NCH * UNITS // 2
U_WO = U_SGU + NCH * UNITS // 2
U_FF = U_WO + NCH * UNITS
U_LAST = U_FF + FULL_GROUPS * GRP_UNITS
NU = U_LAST + J_LAST * 2 * UNITS + NCH * DOWN_LAST

SET0 = dict(z=0, qkv=2, g=4, att=8, sgu=10, wo=12, ff=14)
SET1 = dict(z=0, qkv=2, g=3, att=7, sgu=9, wo=11, ff=13)
N_SET0 = SET0["ff"] + N_J + 2 * (FULL_GROUPS + 1)
N_SET1 = SET1["ff"] + N_J + 2 * (FULL_GROUPS + 1)

T0 = dict(sgu=0, y=2, m=14, h=18, a=22, x=22 + N_J)
T1 = dict(sgu=0, m=2, h=6, a=10, x=10 + N_J)
N_T0, N_T1 = T0["x"] + 4, T1["x"] + 4
N_PRE = 4
N_STR = 7
N_SP = 16
N_CP = 20
N_TILES = 12
N_SAVE = 8
B_SET0, B_SET1 = 8, 7

TILES = [(0, 4, 0, P), (1, 2, 0, 2 * P), (1, 2, 2, 2 * P)]
S_AT, NORM_AT, PT_AT, PV_AT = (1, 5, 9), (3, 7, 11), (5, 9, 13), (7, 11, 15)
Q1_AT = (2, 3)

G_N1, G_N2 = 0, DEPTH * KB
G_SB = G_N2 + DEPTH * KB
G_ROWS = G_SB + DEPTH * GROUPS

TWO_PI = 2 * math.pi
PI_PARTS = []
_rest = TWO_PI
for _ in range(3):
    _scale = 2.0 ** (7 - math.floor(math.log2(_rest)))
    PI_PARTS.append(math.floor(_rest * _scale) / _scale)
    _rest -= PI_PARTS[-1]
PI_PARTS.append(_rest)
MAGIC = 1.5 * 2.0**23
COARSE = 4096.0
TRIG_ANGLE = 10 + 3 * len(PI_PARTS)
PI_IN = 3.1415925


class Steps:

    def __init__(self, eng, sem, per_call):
        self.eng, self.sem, self.per_call = eng, sem, per_call

    def begin(self, call):
        self.base, self.k = call * self.per_call, 0

    def __call__(self, ins, wait=True):
        self.k += 1
        ins.then_inc(self.sem, 1)
        if wait:
            self.eng.wait_ge(self.sem, self.base + self.k)

    def end(self):
        assert self.k == self.per_call, (self.k, self.per_call)


def trunk(nc, x, positions, norm1_g, w_in, b_in, sinks, sgu_ln_g, sgu_ln_b, sgu_w, sgu_b,
          w_attn_branch, w_sgu_branch, w_out, norm2_g, w_gate_up, w_down, final_g, out):
    ctx = ExitStack()
    with ctx:
        at = [(nc.sbuf_base + 63) // 64 * 64]

        def sb(name, shape, dt=F32, offset=None):
            if offset is None:
                offset = at[0]
                at[0] += (math.prod(shape[1:]) * 4 + 31) // 32 * 32
                assert at[0] <= nc.sbuf_usable_end, name
            return nc.alloc_sbuf_tensor_at(name, shape, dt, offset=offset)

        def psum(name, shape):
            return ctx.enter_context(nc.psum_tensor(name, shape, F32))

        def sem(name):
            return ctx.enter_context(nc.semaphore(name))

        raw = sb("raw", [P, SLOTS, KB_U, N])
        w_hi = sb("w_hi", [P, SLOTS, KB_U, N], F32R)
        w_lo = sb("w_lo", [P, SLOTS, KB_U, N], F32R)
        a_at = at[0]
        a_hi = sb("a_hi", [P, KB, SEQ], F32R)
        a_lo = sb("a_lo", [P, KB, SEQ], F32R)
        b_at = at[0]
        b_hi = sb("b_hi", [P, KB, SEQ], F32R)
        b_lo = sb("b_lo", [P, KB, SEQ], F32R)
        c_at = at[0]
        c_hi = sb("c_hi", [P, KB, SEQ], F32R)
        c_lo = sb("c_lo", [P, KB, SEQ], F32R)
        fin_g = sb("fin_g", [P, D], F32, offset=b_at)
        fin_sq = sb("fin_sq", [P, TB, D], F32, offset=a_at)
        gates = sb("gates", [P, TB, 2 * D], F32, offset=c_at)
        ln_gb = sb("ln_gb", [P, 2, W_SGU], F32, offset=c_at)
        ws = sb("ws", [P, GROUPS, P], F32, offset=c_at + 8 * W_SGU)
        ws_t = sb("ws_t", [P, GROUPS, P], F32, offset=c_at + 8 * W_SGU + 4 * GROUPS * P)
        v_sq = sb("v_sq", [P, TB, W_SGU], F32, offset=c_at + 8 * W_SGU + 8 * GROUPS * P)
        h = sb("h", [P, TB, D])
        z = sb("z", [P, TB, 2 * W_SGU])
        q_t = sb("q_t", [P, HQ // 2, SEQ])
        k_z = sb("k_z", [P, HKV, 2, SEQ])
        v_s = sb("v_s", [P, TB, HKV * DH])
        q_g = sb("q_g", [P, 2, SEQ])
        st = sb("st", [P, TB, N])
        gst_at = at[0]
        gst = sb("gst", [P, TB, N])
        scores = sb("scores", [P, N])
        probs = sb("probs", [P, N])
        pt_hi = sb("pt_hi", [P, N], F32R)
        pt_lo = sb("pt_lo", [P, N], F32R, offset=gst_at)
        v_hi = sb("v_hi", [P, TB, 2 * DH], F32R)
        v_lo = sb("v_lo", [P, TB, 2 * DH], F32R)
        bias = sb("bias", [P, 2, N])
        ident = sb("ident", [P, P])
        mask0 = sb("mask0", [P, P])
        mask1 = sb("mask1", [P, 2 * P])
        grow = sb("grow", [P, P])
        gain = sb("gain", [P, G_ROWS])
        sink = sb("sink", [P, DEPTH * HQ])
        pos_i = sb("pos_i", [P, TB], I32)
        pos_f = sb("pos_f", [P, TB])
        freq = sb("freq", [P, HALF])
        ang = sb("ang", [P, TB, HALF])
        turns = sb("turns", [P, TB, HALF])
        turns_hi = sb("turns_hi", [P, TB, HALF])
        sin_h = sb("sin_h", [P, TB, HALF])
        sin = sb("sin", [P, TB, HALF])
        cos = sb("cos", [P, TB, HALF])
        rot = sb("rot", [P, 4, TB * 8 * HALF])
        ss_x, ss_h = sb("ss_x", [P, TB]), sb("ss_h", [P, TB])
        rs_x, rs_h = sb("rs_x", [P, TB]), sb("rs_h", [P, TB])
        ss_last = sb("ss_last", [P, TB])
        mhalf = sb("mhalf", [P, TB])
        v_sum, v_ss, v_nmu, v_rs = (sb(f"v{i}", [P, TB]) for i in range(4))
        mx, nmx, sd, es, den, dsum, rden = (sb(f"sm{i}", [P, GQ]) for i in range(7))

        acc = psum("acc", [P, 2, TB, N])
        tps = [psum(f"tps{b}", [P, N]) for b in range(2)]
        small = psum("small", [P, N])
        cps = psum("cps", [P, N])

        raw_landed = [sem(f"raw_landed{s}") for s in range(SLOTS)]
        bias_landed = [sem(f"bias_landed{s}") for s in range(2)]
        x_landed = [sem(f"x_landed{c}") for c in range(NCH)]
        x0_landed = sem("x0_landed")
        rows_landed, sink_landed, pos_landed = sem("rows_landed"), sem("sink_landed"), sem("pos_landed")
        ln_landed, ws_landed, fin_landed, stored = sem("ln_landed"), sem("ws_landed"), sem("fin_landed"), sem("stored")
        hi_done = sem("hi_done")
        lo_done = sem("lo_done")
        unit_used = sem("unit_used")
        set_read = [sem(f"set_read{s}") for s in range(2)]
        st_ready = sem("st_ready")
        t_done = [sem(f"t_done{b}") for b in range(2)]
        t_hi = [sem(f"t_hi{b}") for b in range(2)]
        t_lo = [sem(f"t_lo{b}") for b in range(2)]
        small_done, small_read = sem("small_done"), sem("small_read")
        cp_done, cp_read = sem("cp_done"), sem("cp_read")
        pt_ready = sem("pt_ready")
        probs_ready = sem("probs_ready")
        qg_ready = sem("qg_ready")
        vg_ready = sem("vg_ready")
        soft = sem("soft")
        exp_done = sem("exp_done")
        den_step = sem("den_step")
        h_saved = sem("h_saved")
        ss_done = sem("ss_done")
        rs_step, rs_ready = sem("rs_step"), sem("rs_ready")
        gelu_v, gelu_u = sem("gelu_v"), sem("gelu_u")
        mu_ready, vss_done = sem("mu_ready"), sem("vss_done")
        lnr_step, lnr_ready = sem("lnr_step"), sem("lnr_ready")
        ln_step = sem("ln_step")
        sgu_y = sem("sgu_y")
        rope_step = sem("rope_step")
        silu_done, sig_done = sem("silu_done"), sem("sig_done")
        ws_masked = sem("ws_masked")
        const_step, consts = sem("const_step"), sem("consts")
        trig, sin_done = sem("trig"), sem("sin_done")
        rows_done = sem("rows_done")
        fin_step, fin_act = sem("fin_step"), sem("fin_act")

        def y_rows(e, heads):
            return tps[0][e * DH:(e + 1) * DH, 0:heads * P].rearrange("p (k e q) -> p k e q", e=2, q=P)[:, :, e]

        def y_place(buf, e, g, t):
            qb, heads, h0, _ = TILES[t]
            return buf[e * DH:(e + 1) * DH, bass.ds(g * 2 + h0 // 2, heads // 2), qb * P:(qb + 1) * P]

        def not_negative(v):
            return nc.s_assert_within(v, 0, None, skip_runtime_bounds_check_because="j > 0 here")

        block = ctx.enter_context(nc.Block())
        pos = positions.rearrange("a (t p) -> p (a t)", p=P)
        x_d = x.rearrange("a (t p) d -> p (a t) d", p=P)
        out_d = out.rearrange("a (t p) d -> p (a t) d", p=P)

        @block.sync
        def _(sp):
            def dma(dst, src, done):
                return sp.dma_start(dst, src).then_inc(done, 16)

            def load_bias(s, k, l, col):
                prev = sp.snap(k + 1)
                sp.wait_ge(set_read[s], prev)
                dma(bias[:, s], b_in[bass.ds(l, 1), bass.ds(col, N)].broadcast_to([P, N]), bias_landed[s])

            def loads(n0, slot0, units, w, l, row0, col):
                for u in range(units):
                    slot = (slot0 + u) % SLOTS
                    free = sp.snap(n0 + u + 1)
                    src = w[bass.ds(l, 1), bass.ds(row0 + u * KB_U * P, KB_U * P), bass.ds(col, N)]
                    sp.wait_ge(lo_done, free)
                    dma(raw[:, slot], src.rearrange("l (k p) n -> p (l k) n", p=P), raw_landed[slot])
                    yield u

            def stream(*block):
                for _ in loads(*block):
                    pass

            def load_x(c):
                dma(h[:, :, c * N:(c + 1) * N], x_d[:, :, c * N:(c + 1) * N], x_landed[c])

            dma(h[:, :, 0:N // 2], x_d[:, :, 0:N // 2], x_landed[0])

            with sp.Fori(0, DEPTH) as l:
                nl = sp.snap(l * NU)
                with sp.Fori(0, 2) as i:
                    for b in range(2):
                        col = i * (-2 * N) + (OFF_Z + (2 + b) * N)
                        for u in loads(nl + U_Z + (2 * i + b) * UNITS, 0, UNITS, w_in, l, 0, col):
                            if b == 0 and u < NCH:
                                with sp.If(l * 2 + i == 0):
                                    if u == 0:
                                        dma(h[:, :, N // 2:N], x_d[:, :, N // 2:N], x0_landed)
                                    else:
                                        load_x(u)
                            if b == 0 and u == 4:
                                with sp.If(l * 2 + i == 0):
                                    sp.dma_start(pos_i[:], pos, allow_slow_non_contiguous=True).then_inc(pos_landed, 16)
                                    dma(sink[:], sinks.rearrange("(a l) h -> a (l h)", a=1).broadcast_to([P, DEPTH * HQ]),
                                        sink_landed)
                            if u == 5:
                                load_bias(b, l * (N_SET1 if b else N_SET0) + i, l, col)
                    with sp.If(i == 0):
                        first = sp.snap(nl + SLOTS + UNITS)
                        sp.wait_ge(unit_used, first)
                        dma(ln_gb[:, 0], sgu_ln_g[bass.ds(l, 1), :].broadcast_to([P, W_SGU]), ln_landed)
                        dma(ln_gb[:, 1], sgu_ln_b[bass.ds(l, 1), :].broadcast_to([P, W_SGU]), ln_landed)
                        dma(ws[:], sgu_w[bass.ds(l, 1)].rearrange("l g t s -> t (l g) s"), ws_landed)
                for u in loads(nl + U_QKV, 0, UNITS, w_in, l, 0, OFF_K):
                    if u == 3:
                        load_bias(0, l * N_SET0 + SET0["qkv"], l, OFF_K)
                with sp.Fori(0, 2) as i:
                    for u in loads(nl + (U_QKV + UNITS) + i * UNITS, 0, UNITS, w_in, l, 0, i * N + OFF_Q):
                        if u == 3:
                            with sp.If(i == 0):
                                load_bias(1, l * N_SET1 + SET1["qkv"], l, i * N + OFF_Q)
                            with sp.Else():
                                load_bias(0, l * N_SET0 + (SET0["qkv"] + 1), l, i * N + OFF_Q)
                with sp.Fori(0, NCH) as g:
                    for b in range(2):
                        at_set = l * N_SET1 + SET1["g"] if b else l * N_SET0 + SET0["g"]
                        col = g * N + (OFF_G + b * D)
                        for u in loads(nl + U_G + (b * UNITS) + g * (2 * UNITS), 0, UNITS, w_in, l, 0, col):
                            if u == 3:
                                load_bias(b, at_set + g, l, col)
                with sp.Fori(0, NCH) as c:
                    stream(nl + U_ATT + c * (UNITS // 2), 0, UNITS // 2, w_attn_branch, l, 0, c * N)
                with sp.Fori(0, NCH) as c:
                    stream(nl + U_SGU + c * (UNITS // 2), 0, UNITS // 2, w_sgu_branch, l, 0, c * N)
                with sp.Fori(0, NCH) as c:
                    stream(nl + U_WO + c * UNITS, 0, UNITS, w_out, l, 0, c * N)

                def ffn_group(n0, j0, n_j, units):
                    with sp.Fori(0, n_j) as j:
                        nj = sp.snap(n0 + j * (2 * UNITS))
                        stream(nj, 0, UNITS, w_gate_up, l, 0, j * N + j0 * N)
                        stream(nj + UNITS, 0, UNITS, w_gate_up, l, 0, j * N + j0 * N + DFF)
                    with sp.Fori(0, 2) as i:
                        nd = sp.snap(n0 + n_j * 2 * UNITS + i * (2 * units))
                        for b in range(2):
                            stream(nd + b * units, b * units, units, w_down, l, j0 * N, i * (2 * N) + b * N)

                with sp.Fori(0, FULL_GROUPS) as f:
                    ffn_group(nl + U_FF + f * GRP_UNITS, f * FJ, FJ, UNITS)
                ffn_group(nl + U_LAST, FULL_GROUPS * FJ, J_LAST, DOWN_LAST)

            sp.wait_ge(unit_used, DEPTH * NU + (SLOTS - NCH * DOWN_LAST))
            dma(fin_g[:], final_g.rearrange("(a n) -> a n", a=1).broadcast_to([P, D]), fin_landed)
            for half in range(2):
                cols = slice(half * D // 2, (half + 1) * D // 2)
                sp.wait_ge(fin_step, 2 + half + 1)
                dma(out_d[:, 0, cols], z[:, 0, cols], stored)
                sp.wait_ge(fin_act, half + 1)
                dma(out_d[:, 1, cols], z[:, 1, cols], stored)
            sp.wait_ge(stored, 16 * 2 * TB)

        @block.gpsimd
        def _(pool):
            k = 0

            def step(ins):
                nonlocal k
                k += 1
                ins.then_inc(const_step, 1)
                pool.wait_ge(const_step, k)

            step(nc.gpsimd.memset(ident[:], 0.0))
            step(nc.gpsimd.affine_select(out=ident[:], in_=ident[:], compare_op=ALU.not_equal, fill=1.0,
                                         base=0, pattern=[[-1, P]], channel_multiplier=1))
            pool.sem_inc(consts, 1)
            step(nc.gpsimd.memset(mask0[:], 0.0))
            step(nc.gpsimd.memset(mask1[:], 0.0))
            step(nc.gpsimd.memset(mhalf[:], -0.5))
            step(nc.gpsimd.affine_select(out=mask0[:], in_=mask0[:], compare_op=ALU.is_ge, fill=NEG,
                                         base=0, pattern=[[-1, P]], channel_multiplier=1))
            step(nc.gpsimd.affine_select(out=mask1[:, P:], in_=mask1[:, P:], compare_op=ALU.is_ge, fill=NEG,
                                         base=0, pattern=[[-1, P]], channel_multiplier=1))
            step(nc.gpsimd.affine_select(out=mask1[:, :P], in_=mask1[:, :P], compare_op=ALU.is_gt, fill=NEG,
                                         base=0, pattern=[[1, P]], channel_multiplier=-1))
            step(nc.gpsimd.memset(k_z[:], 0.0))
            pool.sem_inc(consts, 1)

            def inv_sqrt(to, sums, n, step_sem, k, ready):
                nc.gpsimd.tensor_scalar(to[:], sums[:], 1.0 / n, EPS, ALU.mult, ALU.add).then_inc(step_sem, 1)
                pool.wait_ge(step_sem, k)
                nc.gpsimd.tensor_tensor(to[:], to[:], mhalf[:], ALU.pow).then_inc(ready, 1)

            for l in range(DEPTH):
                pool.wait_ge(ss_done, 2 * l + 1)
                inv_sqrt(rs_x, ss_x, D, rs_step, 2 * l + 1, rs_ready)
                pool.wait_ge(ws_landed, 16 * l + 16)
                nc.gpsimd.affine_select(out=ws[:], in_=ws[:], compare_op=ALU.is_ge, fill=0.0, base=0,
                                        pattern=[[0, GROUPS], [-1, P]], channel_multiplier=1).then_inc(ws_masked, 1)
                pool.wait_ge(vss_done, l + 1)
                inv_sqrt(v_rs, v_ss, W_SGU, lnr_step, l + 1, lnr_ready)
                pool.wait_ge(ss_done, 2 * l + 2)
                inv_sqrt(rs_h, ss_h, D, rs_step, 2 * l + 2, rs_ready)
            pool.wait_ge(ss_done, 2 * DEPTH + 1)
            nc.gpsimd.tensor_tensor(ss_x[:], ss_x[:], ss_last[:], ALU.add).then_inc(rs_step, 1)
            pool.wait_ge(rs_step, 2 * DEPTH + 1)
            inv_sqrt(rs_x, ss_x, D, rs_step, 2 * DEPTH + 2, rs_ready)

        @block.tensor
        def _(pe):
            def products(n0, slot0, units, hi, lo, kb0, s, k, ready=None):
                for u in range(units):
                    yield u
                    if u == 0:
                        pe.wait_ge(set_read[s], k + 1)
                    if ready is not None:
                        ready(u)
                    pe.wait_ge(lo_done, n0 + (u + SLOTS + 1))
                    slot = (slot0 + u) % SLOTS
                    for q in range(KB_U):
                        kb = KB_U * u + q
                        for tb in range(TB):
                            toks = slice(tb * P, (tb + 1) * P)
                            for part, (left, right) in enumerate(((hi, w_hi), (hi, w_lo), (lo, w_hi))):
                                mm = nc.tensor.matmul(acc[:, s, tb], left[:, kb0 + kb, toks], right[:, slot, q],
                                                      start=(kb == 0 and part == 0),
                                                      stop=(kb == units * KB_U - 1 and part == 2))
                    mm.then_inc(unit_used, 1)

            def operand(j0, j1):
                def ready(u):
                    pe.wait_ge(t_lo[u % 2], (j1 if u % 2 else j0) + (u // 2 + 2))
                return ready

            def t_half(b, j, src):
                pe.wait_ge(t_lo[b], j + 1)
                for q in range(2):
                    for tb in range(TB):
                        col = (2 * b + q) * P
                        mm = nc.tensor.transpose(tps[b][:, (q * TB + tb) * P:(q * TB + tb + 1) * P],
                                                 src[:, tb, col:col + P], ident[:])
                mm.then_inc(t_done[b], 1)

            def t_pair(j0, j1, src):
                t_half(0, j0, src)
                t_half(1, j1, src)

            def copied(job, srcs):
                pe.wait_ge(cp_read, job + 1)
                for n, src in enumerate(srcs):
                    mm = nc.tensor.transpose(cps[:, n * P:(n + 1) * P], src, ident[:])
                mm.then_inc(cp_done, 1)

            pe.sem_inc(unit_used, SLOTS)
            pe.wait_ge(consts, 1)
            pe.wait_ge(rows_landed, 16 * 3)
            nc.tensor.transpose(small[:, 0:G_ROWS], grow[0:G_ROWS, :], ident[0:G_ROWS, 0:G_ROWS]).then_inc(rows_done, 1)
            pe.wait_ge(x_landed[0], 16)
            t_half(0, 0, h)
            pe.wait_ge(x0_landed, 16)
            t_half(1, 0, h)

            def t_x(c):
                pe.wait_ge(x_landed[c], 16)
                t_pair(c, c, h[:, :, c * N:(c + 1) * N])

            with pe.Fori(0, DEPTH) as l:
                nl = pe.snap(l * NU)
                s0, s1 = pe.snap(l * N_SET0), pe.snap(l * N_SET1)
                j0, j1 = pe.snap(l * N_T0 + N_PRE), pe.snap(l * N_T1 + N_PRE)
                cp, sm, tiles = pe.snap(l * N_CP), pe.snap(l * N_SP), pe.snap(l * N_TILES)

                with pe.Fori(0, 2) as i:
                    ni = nl + U_Z + i * (2 * UNITS)
                    for u in products(ni, 0, UNITS, a_hi, a_lo, 0, 0, s0 + i, operand(j0 - 4, j1 - 4)):
                        if u in (0, 2):
                            with pe.If(l * 2 + i == 0):
                                t_x(1 + u // 2)
                        if u == 4:
                            with pe.If(i == 0):
                                pe.wait_ge(set_read[1], s1 + 1)
                                t_pair(j0 - 1, j1 - 1, st)
                    for u in products(ni + UNITS, 0, UNITS, a_hi, a_lo, 0, 1, s1 + i):
                        pass

                def gmlp(j):
                    hh, tb = divmod(j, 2)
                    pe.wait_ge(small_read, sm + (j + 1))
                    for g in range(4):
                        col = W_SGU + (4 * hh + g) * P
                        mm = nc.tensor.matmul(small[:, g * P:(g + 1) * P], ws_t[:, 4 * hh + g], z[:, tb, col:col + P],
                                              start=True, stop=True)
                    mm.then_inc(small_done, 1)

                def gmlp_t(j):
                    hh, tb = divmod(j, 2)
                    b, job = j % 2, (j1 if j % 2 else j0) + j // 2
                    pe.wait_ge(sgu_y, 4 * l + (j + 1))
                    pe.wait_ge(t_lo[b], job + 1)
                    for g in range(4):
                        col = (4 * hh + g) * P
                        mm = nc.tensor.transpose(tps[b][:, g * P:(g + 1) * P], z[:, tb, col:col + P], ident[:])
                    mm.then_inc(t_done[b], 1)

                for u in products(nl + U_QKV, 0, UNITS, a_hi, a_lo, 0, 0, s0 + 2):
                    if u in (2, 4):
                        if u == 2:
                            pe.wait_ge(ws_masked, l + 1)
                        w = (u - 2) // 2
                        copied(cp + w, [ws[:, 4 * w + g] for g in range(4)])
                for u in products(nl + U_QKV + UNITS, 0, UNITS, a_hi, a_lo, 0, 1, s1 + 2):
                    if u in (2, 4):
                        w = (u - 2) // 2
                        pe.wait_ge(st_ready, N_STR * l + 1)
                        copied(cp + (2 + w), [st[:, tb, (2 * w + kb) * P:(2 * w + kb + 1) * P]
                                              for kb in range(2) for tb in range(TB)])
                    if u == 1:
                        pe.wait_ge(ln_step, 4 * l + 4)
                        pe.wait_ge(cp_read, cp + 3)
                    if u % 2 == 1:
                        gmlp(u // 2)
                        if u > 1:
                            gmlp_t(u // 2 - 1)
                for u in products(nl + U_QKV + 2 * UNITS, 0, UNITS, a_hi, a_lo, 0, 0, s0 + 3):
                    if u == 1:
                        gmlp_t(3)
                    if u in (2, 4):
                        w = (u - 2) // 2
                        pe.wait_ge(st_ready, N_STR * l + 2)
                        copied(cp + (4 + w), [st[:, tb, (2 * w + kb) * P:(2 * w + kb + 1) * P]
                                              for kb in range(2) for tb in range(TB)])
                def attention(p, g):
                    for t, (qb, heads, h0, keys) in enumerate(TILES):
                        if p == PT_AT[t]:
                            pe.wait_ge(probs_ready, tiles + g * 3 + (t + 1))
                            copied(cp + g * 3 + (8 + t), [probs[:, (a * (keys // P) + kb) * P:(a * (keys // P) + kb + 1) * P]
                                                          for kb in range(keys // P) for a in range(heads)])
                        if p == PV_AT[t]:
                            if t == 0:
                                pe.wait_ge(vg_ready, HKV * l + g + 1)
                            pe.wait_ge(cp_read, cp + g * 3 + (8 + t + 2))
                            pe.wait_ge(t_lo[0], j0 + g * 3 + (T0["y"] + t + 1))
                            for kb in range(keys // P):
                                cols = slice(kb * heads * P, (kb + 1) * heads * P)
                                for part, (left, right) in enumerate(((v_hi, pt_hi), (v_hi, pt_lo), (v_lo, pt_hi))):
                                    mm = nc.tensor.matmul(tps[0][:, 0:heads * P], left[:, kb], right[:, cols],
                                                          start=(kb == 0 and part == 0),
                                                          stop=(kb == keys // P - 1 and part == 2))
                            mm.then_inc(t_done[0], 1)
                    for t, (qb, heads, h0, keys) in enumerate(TILES):
                        if p == S_AT[t]:
                            if t == 0:
                                pe.wait_ge(qg_ready, HKV * l + g + 1)
                            pe.wait_ge(small_read, sm + g * 3 + (4 + t + 1))
                            for a in range(heads):
                                hd = h0 + a
                                k_ap = k_z[:, bass.ds(g, 1), hd % 2, 0:keys].rearrange("p g k -> p (g k)")
                                mm = nc.tensor.matmul(small[:, a * keys:(a + 1) * keys],
                                                      q_g[:, hd // 2, qb * P:(qb + 1) * P], k_ap,
                                                      start=True, stop=True)
                            mm.then_inc(small_done, 1)

                with pe.Fori(0, NCH) as g:
                    ng = nl + U_G + g * (2 * UNITS)
                    for u in products(ng, 0, UNITS, a_hi, a_lo, 0, 0, s0 + SET0["g"] + g):
                        if u in Q1_AT:
                            w = u - Q1_AT[0]
                            with pe.If(g == 0):
                                pe.wait_ge(st_ready, N_STR * l + 3)
                                copied(cp + (6 + w), [st[:, tb, (2 * w + kb) * P:(2 * w + kb + 1) * P]
                                                      for kb in range(2) for tb in range(TB)])
                        attention(u, g)
                    for u in products(ng + UNITS, 0, UNITS, a_hi, a_lo, 0, 1, s1 + SET1["g"] + g):
                        attention(UNITS + u, g)

                with pe.Fori(0, 2) as i:
                    for b in range(2):
                        def ready(u):
                            pe.wait_ge(t_lo[0], j0 + (T0["y"] + 3 * u + 4))
                        for u in products(nl + U_ATT + (2 * i + b) * (UNITS // 2), 0, UNITS // 2, b_hi, b_lo, 0, b,
                                          (s1 + SET1["att"] if b else s0 + SET0["att"]) + i, ready):
                            pass
                with pe.Fori(0, 2) as i:
                    def ready(u):
                        if u == 0:
                            pe.wait_ge(t_lo[1], j1 + (T1["sgu"] + 1 + 2))
                    ni = nl + U_SGU + i * UNITS
                    for u in products(ni, 0, UNITS // 2, b_hi, b_lo, KB // 2, 0, s0 + SET0["sgu"] + i, ready):
                        if u == 2:
                            with pe.If(i == 1):
                                pe.wait_ge(st_ready, N_STR * l + (3 + 2))
                                t_pair(j0 + (T0["m"] + 1), j1 + (T1["m"] + 1), st)
                    for u in products(ni + UNITS // 2, 0, UNITS // 2, b_hi, b_lo, KB // 2, 1, s1 + SET1["sgu"] + i):
                        if u == 2:
                            pe.wait_ge(st_ready, N_STR * l + 2 * i + (3 + 1))
                            t_pair(j0 + T0["m"] + 2 * i, j1 + T1["m"] + 2 * i, st)
                with pe.Fori(0, 2) as i:
                    ni = nl + U_WO + i * (2 * UNITS)
                    for u in products(ni, 0, UNITS, a_hi, a_lo, 0, 0, s0 + SET0["wo"] + i,
                                      operand(j0 + T0["m"], j1 + T1["m"])):
                        if u == 2:
                            with pe.If(i == 0):
                                pe.wait_ge(st_ready, N_STR * l + (3 + 4))
                                t_pair(j0 + (T0["m"] + 3), j1 + (T1["m"] + 3), st)
                            with pe.Else():
                                pe.wait_ge(set_read[1], s1 + (SET1["wo"] + 2))
                                t_pair(j0 + (T0["h"] + 1), j1 + (T1["h"] + 1), st)
                    for u in products(ni + UNITS, 0, UNITS, a_hi, a_lo, 0, 1, s1 + SET1["wo"] + i):
                        if u == 2:
                            pe.wait_ge(set_read[0], s0 + i + (SET0["wo"] + 2))
                            t_pair(j0 + T0["h"] + 2 * i, j1 + T1["h"] + 2 * i, st)

                def ffn_group(n0, m0, d0, n_j, units, last, group):
                    f0, f1 = s0 + SET0["ff"] + d0, s1 + SET1["ff"] + d0
                    with pe.Fori(0, n_j) as j:
                        nj = n0 + j * (2 * UNITS)
                        for u in products(nj, 0, UNITS, b_hi, b_lo, 0, 0, f0 + j,
                                          operand(j0 + T0["h"], j1 + T1["h"])):
                            if u == 2:
                                if not last:
                                    with pe.If(group * FJ + j == 0):
                                        pe.wait_ge(set_read[1], s1 + (SET1["wo"] + 3))
                                        t_pair(j0 + (T0["h"] + 3), j1 + (T1["h"] + 3), st)
                                with pe.If(j != 0):
                                    pe.wait_ge(set_read[1], f1 + j + 1)
                                    t_pair(j0 + T0["a"] + m0 + j - 1, j1 + T1["a"] + m0 + j - 1, st)
                        for u in products(nj + UNITS, 0, UNITS, b_hi, b_lo, 0, 1, f1 + j):
                            pass
                    with pe.Fori(0, 2) as i:
                        nd = n0 + n_j * 2 * UNITS + i * (2 * units)
                        for u in products(nd, 0, units, c_hi, c_lo, 0, 0, f0 + n_j + i,
                                          operand(j0 + T0["a"] + m0, j1 + T1["a"] + m0)):
                            if u == 2:
                                with pe.If(i == 0):
                                    pe.wait_ge(set_read[1], f1 + (n_j + 1))
                                    t_pair(j0 + T0["a"] + m0 + (n_j - 1), j1 + T1["a"] + m0 + (n_j - 1), st)
                                if last:
                                    with pe.If(l * 2 + i == 1):
                                        pe.wait_ge(set_read[1], f1 + (n_j + 2))
                                        t_pair(j0 + (T0["x"] + 1), j1 + (T1["x"] + 1), st)
                        for u in products(nd + units, units, units, c_hi, c_lo, 0, 1, f1 + n_j + i):
                            if u == 2 and last:
                                with pe.If(l != DEPTH - 1):
                                    pe.wait_ge(set_read[0], f0 + i + (n_j + 2))
                                    t_pair(j0 + T0["x"] + 2 * i, j1 + T1["x"] + 2 * i, st)

                with pe.Fori(0, FULL_GROUPS) as f:
                    ffn_group(nl + U_FF + f * GRP_UNITS, f * FJ, f * (FJ + 2), FJ, UNITS, False, f)
                ffn_group(nl + U_LAST, FULL_GROUPS * FJ, FULL_GROUPS * (FJ + 2), J_LAST, DOWN_LAST, True, None)

        @block.scalar
        def _(act):
            def split_hi(n, slot):
                act.wait_ge(raw_landed[slot], (n - slot) * (16 // SLOTS) + 16)
                act.wait_ge(unit_used, n + 1)
                nc.scalar.activation(w_hi[:, slot], raw[:, slot], ACT.Copy).then_inc(hi_done, 1)

            def splitting(n0, slot0, units, stop=None):
                for u in range(units):
                    yield u
                    if stop is not None and u + AHEAD >= units:
                        with act.If(stop != 2 * DEPTH - 1):
                            split_hi(n0 + (u + AHEAD), (slot0 + u + AHEAD) % SLOTS)
                    else:
                        split_hi(n0 + (u + AHEAD), (slot0 + u + AHEAD) % SLOTS)

            def hi_half(b, j, hi, kb0, g0=None):
                act.wait_ge(t_done[b], j + 1)
                if g0 is None:
                    a = nc.scalar.activation(hi[:, bass.ds(kb0 + 2 * b, 2)],
                                             tps[b].rearrange("p (k t) -> p k t", k=2), ACT.Copy)
                else:
                    for q in range(2):
                        a = nc.scalar.activation(hi[:, bass.ds(kb0 + (2 * b + q), 1)],
                                                 tps[b][:, q * SEQ:(q + 1) * SEQ].unsqueeze(1), ACT.Copy,
                                                 scale=gain[:, bass.ds(g0 + (2 * b + q), 1)])
                a.then_inc(t_hi[b], 1)

            def hi_pair(j0, j1, hi, kb0, g0=None):
                hi_half(0, j0, hi, kb0, g0)
                hi_half(1, j1, hi, kb0, g0)

            def save_h(s, k, c):
                act.wait_ge(set_read[s], k + 2)
                nc.scalar.activation(h[:, :, bass.ds(c * N, N)], st[:], ACT.Copy).then_inc(h_saved, 1)

            def sum_squares(to, saved):
                act.wait_ge(h_saved, saved + 1)
                for tb in range(TB):
                    a = nc.scalar.activation(z[:, tb], h[:, tb], ACT.Square, accum_out=to[:, tb:tb + 1])
                a.then_inc(ss_done, 1)

            for s in (cp_read, exp_done, h_saved):
                act.sem_inc(s, 1)
            for to, rows in ((grow[G_N1:G_N2], norm1_g.rearrange("l (k p) -> (l k) p", p=P)),
                             (grow[G_N2:G_SB], norm2_g.rearrange("l (k p) -> (l k) p", p=P)),
                             (grow[G_SB:G_ROWS], sgu_b.rearrange("l g t -> (l g) t"))):
                act.dma_start(to, rows).then_inc(rows_landed, 16)
            split_hi(0, 0)
            act.wait_ge(small_read, 1)
            hi_half(0, 0, a_hi, 0, 0)
            hi_half(1, 0, a_hi, 0, 0)
            for u in range(1, AHEAD):
                split_hi(u, u)

            with act.Fori(0, DEPTH) as l:
                nl = act.snap(l * NU)
                s0, s1 = act.snap(l * N_SET0), act.snap(l * N_SET1)
                j0, j1 = act.snap(l * N_T0 + N_PRE), act.snap(l * N_T1 + N_PRE)
                cp = act.snap(l * N_CP)
                with act.Fori(0, 2) as i:
                    for u in splitting(nl + U_Z + i * (2 * UNITS), 0, UNITS):
                        if u in (0, 2):
                            c = 1 + u // 2
                            with act.If(l * 2 + i == 0):
                                hi_pair(c, c, a_hi, 4 * c, 4 * c)
                        if u == 4:
                            with act.If(i == 0):
                                hi_pair(j0 - 1, j1 - 1, a_hi, KB - 4, l * KB + (KB - 4))
                                sum_squares(ss_x, N_SAVE * l)
                    for u in splitting(nl + U_Z + i * (2 * UNITS) + UNITS, 0, UNITS):
                        if u == 4:
                            with act.If(l * 2 + i == 0):
                                act.wait_ge(trig, TRIG_ANGLE)
                                nc.scalar.activation(sin[:], ang[:], ACT.Sin).then_inc(sin_done, 1)
                                nc.scalar.activation(sin_h[:], ang[:], ACT.Sin, scale=0.5).then_inc(sin_done, 1)
                                act.wait_ge(consts, 2)

                def gelu_steps(u):
                    if u == 1:
                        act.wait_ge(set_read[1], s1 + 3)
                        for tb in range(TB):
                            nc.scalar.activation(z[:, tb, W_SGU:], z[:, tb, W_SGU:], ACT.Gelu,
                                                 accum_out=v_sum[:, tb:tb + 1]).then_inc(gelu_v, 1)
                    if u == 2:
                        for tb in range(TB):
                            nc.scalar.activation(z[:, tb, :W_SGU], z[:, tb, :W_SGU], ACT.Gelu).then_inc(gelu_u, 1)
                    if u == 3:
                        act.wait_ge(mu_ready, l + 1)
                        for tb in range(TB):
                            a = nc.scalar.activation(v_sq[:, tb], z[:, tb, W_SGU:], ACT.Square,
                                                     bias=v_nmu[:, tb:tb + 1], accum_out=v_ss[:, tb:tb + 1])
                        a.then_inc(vss_done, 1)

                def copied(job, to, src=None):
                    act.wait_ge(cp_done, job + 1)
                    nc.scalar.activation(to, cps[:] if src is None else src, ACT.Copy).then_inc(cp_read, 1)

                def gmlp_hi(j):
                    hh, tb = divmod(j, 2)
                    b, job = j % 2, (j1 if j % 2 else j0) + j // 2
                    act.wait_ge(t_done[b], job + 1)
                    nc.scalar.activation(b_hi[:, KB // 2 + 4 * hh:KB // 2 + 4 * hh + 4, tb * P:(tb + 1) * P],
                                         tps[b].rearrange("p (k t) -> p k t", k=4), ACT.Copy).then_inc(t_hi[b], 1)

                for u in splitting(nl + U_QKV, 0, UNITS):
                    gelu_steps(u)
                    if u in (2, 4):
                        w = (u - 2) // 2
                        copied(cp + w, ws_t[:, 4 * w:4 * w + 4], cps.rearrange("p (g t) -> p g t", g=4))
                for u in splitting(nl + U_QKV + UNITS, 0, UNITS):
                    if u in (2, 4):
                        w = (u - 2) // 2
                        act.wait_ge(cp_done, cp + (2 + w + 1))
                        src = cps.rearrange("p (k t) -> p k t", k=2)
                        nc.scalar.activation(k_z[0:DH, w:HKV:2, 0], src[0:DH], ACT.Copy)
                        nc.scalar.activation(k_z[DH:P, 1 - w:HKV:2, 1], src[DH:P], ACT.Copy).then_inc(cp_read, 1)
                    if u % 2 == 1 and u > 1:
                        gmlp_hi(u // 2 - 1)
                for u in splitting(nl + U_QKV + 2 * UNITS, 0, UNITS):
                    if u == 1:
                        gmlp_hi(3)
                    if u in (2, 4):
                        w = (u - 2) // 2
                        copied(cp + (4 + w), q_t[:, 2 * w:2 * w + 2].rearrange("p k t -> p (k t)"))
                def attention(p, g):
                    if p == 0:
                        act.wait_ge(small_done, l * N_SP + g * 3 + 4)
                        act.wait_ge(cp_read, cp + 2 * g + 7)
                        nc.scalar.activation(q_g[:], q_t[:, bass.ds(g * 2, 2)], ACT.Copy)
                        act.wait_ge(t_done[0], j0 + g * 3 + T0["y"])
                        nc.scalar.activation(v_hi[:].rearrange("p t (e d) -> p t e d", e=2),
                                             v_s[:, :, bass.ds(g * DH, DH)].unsqueeze(2).broadcast_to([P, TB, 2, DH]),
                                             ACT.Copy).then_inc(qg_ready, 1)
                    for t, (qb, heads, h0, keys) in enumerate(TILES):
                        if p == PT_AT[t]:
                            act.wait_ge(cp_done, cp + g * 3 + (8 + t + 1))
                            nc.scalar.activation(pt_hi[:], cps[:], ACT.Copy).then_inc(pt_ready, 1)
                        if p == PV_AT[t]:
                            act.wait_ge(t_done[0], j0 + g * 3 + (T0["y"] + t + 1))
                            for e in range(2):
                                a = nc.scalar.activation(y_place(b_hi, e, g, t), y_rows(e, heads), ACT.Copy)
                            a.then_inc(t_hi[0], 1)
                    for t, (qb, heads, h0, keys) in enumerate(TILES):
                        if p == S_AT[t]:
                            act.wait_ge(soft, 4 * (l * N_TILES) + g * 12 + 4 * (t + 1))
                            for a in range(heads):
                                nc.scalar.activation(probs[:, a * keys:(a + 1) * keys], scores[:, a * keys:(a + 1) * keys],
                                                     ACT.Exp, bias=nmx[:, a:a + 1], accum_out=den[:, a:a + 1])
                            nc.scalar.activation(es[:, 0:heads], sd[:, 0:heads], ACT.Exp).then_inc(exp_done, 1)

                with act.Fori(0, NCH) as g:
                    ng = nl + U_G + g * (2 * UNITS)
                    for u in splitting(ng, 0, UNITS):
                        if u in Q1_AT:
                            w = u - Q1_AT[0]
                            with act.If(g == 0):
                                copied(cp + (6 + w), q_t[:, 4 + 2 * w:6 + 2 * w].rearrange("p k t -> p (k t)"))
                        attention(u, g)
                    for u in splitting(ng + UNITS, 0, UNITS):
                        attention(UNITS + u, g)

                with act.Fori(0, 2) as i:
                    for b in range(2):
                        for u in splitting(nl + U_ATT + (2 * i + b) * (UNITS // 2), 0, UNITS // 2):
                            if u in (1, 2):
                                if u == 1:
                                    act.wait_ge(set_read[1], s1 + (SET1["att"] + 1))
                                col = (u - 1) * D + i * (2 * N) + b * N
                                blk = gates[:, :, bass.ds(col, N)]
                                nc.scalar.activation(blk, blk, ACT.Sigmoid).then_inc(sig_done, 1)
                with act.Fori(0, 2) as i:
                    ni = nl + U_SGU + i * UNITS
                    for u in splitting(ni, 0, UNITS // 2):
                        if u == 2:
                            with act.If(i == 1):
                                hi_pair(j0 + (T0["m"] + 1), j1 + (T1["m"] + 1), a_hi, 4)
                    for u in splitting(ni + UNITS // 2, 0, UNITS // 2):
                        if u == 2:
                            hi_pair(j0 + T0["m"] + 2 * i, j1 + T1["m"] + 2 * i, a_hi, 8 * i)
                n2 = G_N2 + l * KB
                with act.Fori(0, 2) as i:
                    ni = nl + U_WO + i * (2 * UNITS)
                    for u in splitting(ni, 0, UNITS):
                        if u == 2:
                            with act.If(i == 0):
                                hi_pair(j0 + (T0["m"] + 3), j1 + (T1["m"] + 3), a_hi, KB - 4)
                            with act.Else():
                                save_h(1, s1 + SET1["wo"], 1)
                                hi_pair(j0 + (T0["h"] + 1), j1 + (T1["h"] + 1), b_hi, 4, n2 + 4)
                    for u in splitting(ni + UNITS, 0, UNITS):
                        if u == 2:
                            save_h(0, s0 + SET0["wo"] + i, 2 * i)
                            hi_pair(j0 + T0["h"] + 2 * i, j1 + T1["h"] + 2 * i, b_hi, 8 * i, n2 + 8 * i)

                def ffn_group(n0, m0, d0, n_j, units, last, group):
                    f0, f1 = s0 + SET0["ff"] + d0, s1 + SET1["ff"] + d0
                    with act.Fori(0, n_j) as j:
                        nj = n0 + j * (2 * UNITS)
                        for u in splitting(nj, 0, UNITS):
                            if u == 2:
                                if not last:
                                    with act.If(group * FJ + j == 0):
                                        save_h(1, s1 + (SET1["wo"] + 1), 3)
                                        hi_pair(j0 + (T0["h"] + 3), j1 + (T1["h"] + 3), b_hi, KB - 4, n2 + (KB - 4))
                                        sum_squares(ss_h, N_SAVE * l + 4)
                                with act.If(j != 0):
                                    hi_pair(j0 + T0["a"] + m0 + j - 1, j1 + T1["a"] + m0 + j - 1, c_hi,
                                            not_negative(4 * j - 4))
                        for u in splitting(nj + UNITS, 0, UNITS):
                            if u == 1:
                                act.wait_ge(set_read[0], f0 + j + 2)
                                nc.scalar.activation(gst[:], gst[:], ACT.Silu).then_inc(silu_done, 1)
                    with act.Fori(0, 2) as i:
                        nd = n0 + n_j * 2 * UNITS + i * (2 * units)
                        for u in splitting(nd, 0, units):
                            if u == 2:
                                with act.If(i == 0):
                                    hi_pair(j0 + T0["a"] + m0 + (n_j - 1), j1 + T1["a"] + m0 + (n_j - 1), c_hi,
                                            4 * (n_j - 1))
                                if last:
                                    with act.If(i == 1):
                                        save_h(1, f1 + n_j, 1)
                                    with act.If(l * 2 + i == 1):
                                        hi_pair(j0 + (T0["x"] + 1), j1 + (T1["x"] + 1), a_hi, 4, (l + 1) * KB + 4)
                        for u in splitting(nd + units, units, units, stop=l * 2 + i if last else None):
                            if u == 2 and last:
                                save_h(0, f0 + n_j + i, 2 * i)
                                with act.If(l != DEPTH - 1):
                                    hi_pair(j0 + T0["x"] + 2 * i, j1 + T1["x"] + 2 * i, a_hi, 8 * i,
                                            (l + 1) * KB + 8 * i)

                with act.Fori(0, FULL_GROUPS) as f:
                    ffn_group(nl + U_FF + f * GRP_UNITS, f * FJ, f * (FJ + 2), FJ, UNITS, False, f)
                ffn_group(nl + U_LAST, FULL_GROUPS * FJ, FULL_GROUPS * (FJ + 2), J_LAST, DOWN_LAST, True, None)
                with act.If(l != DEPTH - 1):
                    save_h(1, s1 + (N_SET1 - 1), 3)

            act.wait_ge(h_saved, N_SAVE * DEPTH)
            for tb in range(TB):
                nc.scalar.activation(fin_sq[:, tb, 0:D - N], h[:, tb, 0:D - N], ACT.Square,
                                     accum_out=ss_x[:, tb:tb + 1])
            act.wait_ge(set_read[1], DEPTH * N_SET1 + 1)
            for tb in range(TB):
                a = nc.scalar.activation(fin_sq[:, tb, D - N:], st[:, tb], ACT.Square, accum_out=ss_last[:, tb:tb + 1])
            a.then_inc(ss_done, 1)
            act.wait_ge(rs_ready, 2 * DEPTH + 1)
            act.wait_ge(fin_step, 2)
            for half in range(2):
                cols = slice(half * D // 2, (half + 1) * D // 2)
                nc.scalar.activation(z[:, 1, cols], z[:, 1, cols], ACT.Copy, scale=rs_x[:, 1:2]).then_inc(fin_act, 1)

        @block.vector
        def _(dve):
            def split_lo(n, slot):
                dve.wait_ge(hi_done, n + 1)
                nc.vector.tensor_tensor(w_lo[:, slot], raw[:, slot], w_hi[:, slot].bitcast(F32),
                                        ALU.subtract).then_inc(lo_done, 1)

            def splitting(n0, slot0, units, stop=None):
                for u in range(units):
                    yield u
                    if stop is not None and u + AHEAD >= units:
                        with dve.If(stop != 2 * DEPTH - 1):
                            split_lo(n0 + (u + AHEAD), (slot0 + u + AHEAD) % SLOTS)
                    else:
                        split_lo(n0 + (u + AHEAD), (slot0 + u + AHEAD) % SLOTS)

            def lo_half(b, j, hi, lo, kb0, g0=None):
                dve.wait_ge(t_hi[b], j + 1)
                if g0 is None:
                    kbs = bass.ds(kb0 + 2 * b, 2)
                    v = nc.vector.tensor_tensor(lo[:, kbs], tps[b].rearrange("p (k t) -> p k t", k=2),
                                                hi[:, kbs].bitcast(F32), ALU.subtract)
                else:
                    for q in range(2):
                        kbs = bass.ds(kb0 + (2 * b + q), 1)
                        v = nc.vector.scalar_tensor_tensor(
                            out=lo[:, kbs], in0=tps[b][:, q * SEQ:(q + 1) * SEQ].unsqueeze(1),
                            scalar=gain[:, bass.ds(g0 + (2 * b + q), 1)], in1=hi[:, kbs].bitcast(F32),
                            op0=ALU.mult, op1=ALU.subtract)
                v.then_inc(t_lo[b], 1)

            def lo_pair(j0, j1, hi, lo, kb0, g0=None):
                lo_half(0, j0, hi, lo, kb0, g0)
                lo_half(1, j1, hi, lo, kb0, g0)

            def evac_proj(s, used, k_bias, dst, done):
                dve.wait_ge(unit_used, used + SLOTS)
                dve.wait_ge(bias_landed[s], 16 * k_bias + 16)
                for tb in range(TB):
                    v = nc.vector.scalar_tensor_tensor(out=dst(tb), in0=acc[:, s, tb], scalar=rs_x[:, tb:tb + 1],
                                                       in1=bias[:, s], op0=ALU.mult, op1=ALU.add)
                v.then_inc(done, 1)

            def evac_residual(s, used, c, to_st, saved=None, j1=None):
                dve.wait_ge(unit_used, used + SLOTS)
                cols = bass.ds(c * N, N)
                if to_st:
                    dve.wait_ge(t_done[1], j1)
                    dve.wait_ge(h_saved, saved + 1)
                nc.vector.tensor_tensor(st[:] if to_st else h[:, :, cols], acc[:, s], h[:, :, cols],
                                        ALU.add).then_inc(set_read[s], 1)

            dve.sem_inc(lo_done, SLOTS)
            for s in (set_read[0], t_lo[0], t_lo[1]):
                dve.sem_inc(s, 1)
            dve.wait_ge(rows_done, 1)
            nc.vector.tensor_copy(gain[:], small[:, 0:G_ROWS]).then_inc(small_read, 1)
            dve.wait_ge(small_read, 1)
            split_lo(0, 0)
            lo_pair(0, 0, a_hi, a_lo, 0, 0)
            for u in range(1, AHEAD):
                split_lo(u, u)
            trig_step = Steps(dve, trig, TRIG_ANGLE + 2)
            trig_step.begin(0)

            def count_turns():
                trig_step(nc.vector.tensor_scalar(turns[:], ang[:], 1.0 / TWO_PI, MAGIC, ALU.mult, ALU.add))
                trig_step(nc.vector.tensor_scalar(turns[:], turns[:], MAGIC, None, ALU.subtract))

            def take_turns(counts):
                for part in PI_PARTS:
                    for count in counts:
                        trig_step(nc.vector.scalar_tensor_tensor(out=ang[:], in0=count[:], scalar=-part, in1=ang[:],
                                                                 op0=ALU.mult, op1=ALU.add))

            def angles(u):
                if u == 1:
                    for f in range(HALF):
                        v = nc.vector.memset(freq[:, f:f + 1], float(np.float32(THETA ** (-f / HALF))))
                    dve.wait_ge(pos_landed, 16)
                    trig_step(nc.vector.tensor_copy(pos_f[:], pos_i[:]))
                    trig_step(nc.vector.tensor_tensor(ang[:], pos_f[:].unsqueeze(2).broadcast_to([P, TB, HALF]),
                                                      freq[:].unsqueeze(1).broadcast_to([P, TB, HALF]), ALU.mult))
                    count_turns()
                    trig_step(nc.vector.tensor_scalar(turns_hi[:], turns[:], 1.0 / COARSE, MAGIC, ALU.mult, ALU.add))
                    trig_step(nc.vector.tensor_scalar(turns_hi[:], turns_hi[:], MAGIC, COARSE, ALU.subtract, ALU.mult))
                    trig_step(nc.vector.tensor_tensor(turns[:], turns[:], turns_hi[:], ALU.subtract))
                if u == 2:
                    take_turns((turns_hi, turns))
                if u == 3:
                    count_turns()
                    take_turns((turns,))
                    trig_step(nc.vector.tensor_scalar(ang[:], ang[:], PI_IN, -PI_IN, ALU.min, ALU.max))

            def cosine():
                dve.wait_ge(sin_done, 2)
                trig_step(nc.vector.tensor_tensor(cos[:], sin_h[:], sin_h[:], ALU.mult))
                trig_step(nc.vector.tensor_scalar(cos[:], cos[:], -2.0, 1.0, ALU.mult, ALU.add))
                dve.wait_ge(consts, 2)
                dve.wait_ge(sink_landed, 16)
                trig_step.end()

            rope_steps = Steps(dve, rope_step, 6)
            with dve.Fori(0, DEPTH) as l:
                nl = dve.snap(l * NU)
                s0, s1 = dve.snap(l * N_SET0), dve.snap(l * N_SET1)
                j0, j1 = dve.snap(l * N_T0 + N_PRE), dve.snap(l * N_T1 + N_PRE)
                cp, sm, tiles = dve.snap(l * N_CP), dve.snap(l * N_SP), dve.snap(l * N_TILES)
                bias0, bias1 = dve.snap(l * B_SET0), dve.snap(l * B_SET1)
                with dve.Fori(0, 2) as i:
                    ni = nl + U_Z + i * (2 * UNITS)
                    for u in splitting(ni, 0, UNITS):
                        if u == 0:
                            with dve.If(i == 1):
                                evac_proj(1, ni, bias1, lambda tb: z[:, tb, 3 * N:4 * N], set_read[1])
                        if u in (0, 2):
                            c = 1 + u // 2
                            with dve.If(l * 2 + i == 0):
                                lo_pair(c, c, a_hi, a_lo, 4 * c, 4 * c)
                                if u == 2:
                                    dve.wait_ge(x_landed[NCH - 1], 16)
                                    nc.vector.tensor_copy(st[:], h[:, :, D - N:]).then_inc(set_read[1], 1)
                        if u == 4:
                            with dve.If(i == 0):
                                lo_pair(j0 - 1, j1 - 1, a_hi, a_lo, KB - 4, l * KB + (KB - 4))
                    for u in splitting(ni + UNITS, 0, UNITS):
                        if u in (1, 2, 3, 6):
                            with dve.If(l * 2 + i == 0):
                                if u < 4:
                                    angles(u)
                                else:
                                    cosine()
                        if u == 0:
                            dve.wait_ge(rs_ready, 2 * l + 1)
                            evac_proj(0, ni + UNITS, bias0 + i,
                                      lambda tb: z[:, tb, bass.ds(2 * N - i * (2 * N), N)], set_read[0])

                def rope(call, heads):
                    rope_steps.begin(call)
                    hd = st[:, :, 0:heads * DH].rearrange("p t (h d) -> p t h d", d=DH)
                    t1, t2 = hd[:, :, :, 0:HALF], hd[:, :, :, HALF:ROPE]
                    c_, s_ = (a[:].unsqueeze(2).broadcast_to([P, TB, heads, HALF]) for a in (cos, sin))
                    tmp = [rot[:, n, 0:TB * heads * HALF].rearrange("p (t h d) -> p t h d", t=TB, h=heads)
                           for n in range(4)]
                    for n, (t, f) in enumerate(((t1, c_), (t2, s_), (t2, c_), (t1, s_))):
                        rope_steps(nc.vector.tensor_tensor(tmp[n], t, f, ALU.mult), wait=(n == 3))
                    rope_steps(nc.vector.tensor_tensor(t1, tmp[0], tmp[1], ALU.subtract), wait=False)
                    rope_steps(nc.vector.tensor_tensor(t2, tmp[2], tmp[3], ALU.add))
                    rope_steps.end()

                def layer_norm(u):
                    if u == 3:
                        dve.wait_ge(gelu_v, 2 * l + 2)
                        nc.vector.tensor_scalar(v_nmu[:], v_sum[:], -1.0 / W_SGU, None, ALU.mult).then_inc(mu_ready, 1)
                    if u in (5, 6):
                        tb = u - 5
                        if tb == 0:
                            dve.wait_ge(ln_landed, 32 * l + 32)
                            dve.wait_ge(lnr_ready, l + 1)
                            dve.wait_ge(mu_ready, l + 1)
                        v = z[:, tb, W_SGU:]
                        nc.vector.scalar_tensor_tensor(out=v, in0=v, scalar=v_nmu[:, tb:tb + 1], in1=ln_gb[:, 0],
                                                       op0=ALU.add, op1=ALU.mult).then_inc(ln_step, 1)
                    if u == 7:
                        dve.wait_ge(ln_step, 4 * l + 2)
                        for tb in range(TB):
                            v = z[:, tb, W_SGU:]
                            nc.vector.scalar_tensor_tensor(out=v, in0=v, scalar=v_rs[:, tb:tb + 1], in1=ln_gb[:, 1],
                                                           op0=ALU.mult, op1=ALU.add).then_inc(ln_step, 1)

                def gmlp(j):
                    hh, tb = divmod(j, 2)
                    dve.wait_ge(small_done, sm + (j + 1))
                    v = z[:, tb, W_SGU + hh * N:W_SGU + (hh + 1) * N].rearrange("p (g c) -> p g c", g=4)
                    sb_col = gain[:, bass.ds(G_SB + 4 * hh + l * GROUPS, 4)].unsqueeze(2).broadcast_to([P, 4, P])
                    nc.vector.tensor_tensor(v, small.rearrange("p (g c) -> p g c", g=4), sb_col,
                                            ALU.add).then_inc(small_read, 1)
                    dve.wait_ge(small_read, sm + (j + 2))
                    dve.wait_ge(gelu_u, 2 * l + 2)
                    uu = z[:, tb, hh * N:(hh + 1) * N]
                    nc.vector.tensor_tensor(uu, uu, z[:, tb, W_SGU + hh * N:W_SGU + (hh + 1) * N],
                                            ALU.mult).then_inc(sgu_y, 1)

                def gmlp_lo(j):
                    hh, tb = divmod(j, 2)
                    b, job = j % 2, (j1 if j % 2 else j0) + j // 2
                    dve.wait_ge(t_hi[b], job + 1)
                    to = (slice(None), slice(KB // 2 + 4 * hh, KB // 2 + 4 * hh + 4), slice(tb * P, (tb + 1) * P))
                    nc.vector.tensor_tensor(b_lo[to], tps[b].rearrange("p (k t) -> p k t", k=4),
                                            b_hi[to].bitcast(F32), ALU.subtract).then_inc(t_lo[b], 1)

                for u in splitting(nl + U_QKV, 0, UNITS):
                    if u == 0:
                        evac_proj(1, nl + U_QKV, bias1 + 1, lambda tb: z[:, tb, N:2 * N], set_read[1])
                    layer_norm(u)
                for u in splitting(nl + U_QKV + UNITS, 0, UNITS):
                    if u == 0:
                        dve.wait_ge(unit_used, nl + (U_QKV + UNITS + SLOTS))
                        dve.wait_ge(bias_landed[0], 16 * bias0 + 16 * 3)
                        dve.wait_ge(t_done[1], j1)
                        dve.wait_ge(h_saved, N_SAVE * l + 1)
                        dve.wait_ge(qg_ready, HKV * l)
                        kw = HKV * DH
                        for to, cols in ((st, slice(0, kw)), (v_s, slice(kw, 2 * kw))):
                            for tb in range(TB):
                                v = nc.vector.scalar_tensor_tensor(
                                    out=to[:, tb, 0:kw], in0=acc[:, 0, tb, cols], scalar=rs_x[:, tb:tb + 1],
                                    in1=bias[:, 0, cols], op0=ALU.mult, op1=ALU.add)
                        v.then_inc(set_read[0], 1)
                        dve.wait_ge(set_read[0], s0 + 4)
                        rope(3 * l, HKV)
                        kh = st[:].rearrange("p t (w k e d) -> p w t k e d", w=2, k=2, e=2)
                        for e in range(2):
                            v = nc.vector.tensor_copy(kh[:, 1, :, :, e], kh[:, 0, :, :, 1 - e])
                        v.then_inc(st_ready, 1)
                    if u % 2 == 1:
                        gmlp(u // 2)
                        if u > 1:
                            gmlp_lo(u // 2 - 1)

                def evac_q(s, used, k_bias, copied_jobs, call, k):
                    dve.wait_ge(cp_done, copied_jobs)
                    evac_proj(s, used, k_bias, lambda tb: st[:, tb], set_read[s])
                    dve.wait_ge(set_read[s], k + 2)
                    rope(call, 8)
                    dve.sem_inc(st_ready, 1)

                for u in splitting(nl + U_QKV + 2 * UNITS, 0, UNITS):
                    if u == 0:
                        evac_q(1, nl + (U_QKV + 2 * UNITS), bias1 + 2, cp + 4, 3 * l + 1, s1 + 2)
                    if u == 1:
                        gmlp_lo(3)
                def attention(p, g):
                    if p == 2:
                        dve.wait_ge(qg_ready, HKV * l + g + 1)
                        dve.wait_ge(t_done[0], j0 + g * 3 + T0["y"])
                        view = "p t (e d) -> p t e d"
                        nc.vector.tensor_tensor(v_lo[:].rearrange(view, e=2),
                                                v_s[:, :, bass.ds(g * DH, DH)].unsqueeze(2).broadcast_to([P, TB, 2, DH]),
                                                v_hi[:].bitcast(F32).rearrange(view, e=2),
                                                ALU.subtract).then_inc(vg_ready, 1)
                    for t, (qb, heads, h0, keys) in enumerate(TILES):
                        if p == NORM_AT[t]:
                            dve.wait_ge(exp_done, tiles + g * 3 + (t + 2))
                            nc.vector.tensor_tensor(dsum[:, 0:heads], den[:, 0:heads], es[:, 0:heads],
                                                    ALU.add).then_inc(den_step, 1)
                            dve.wait_ge(den_step, 2 * tiles + 6 * g + (2 * t + 1))
                            nc.vector.reciprocal(rden[:, 0:heads], dsum[:, 0:heads]).then_inc(den_step, 1)
                            dve.wait_ge(den_step, 2 * tiles + 6 * g + (2 * t + 2))
                            pr = probs[:].rearrange("p (h k) -> p h k", h=heads)
                            nc.vector.tensor_tensor(pr, pr, rden[:, 0:heads].unsqueeze(2).broadcast_to([P, heads, keys]),
                                                    ALU.mult).then_inc(probs_ready, 1)
                        if p == PT_AT[t]:
                            dve.wait_ge(pt_ready, tiles + g * 3 + (t + 1))
                            nc.vector.tensor_tensor(pt_lo[:], cps[:], pt_hi[:].bitcast(F32),
                                                    ALU.subtract).then_inc(cp_read, 1)
                        if p == PV_AT[t]:
                            dve.wait_ge(t_hi[0], j0 + g * 3 + (T0["y"] + t + 1))
                            for e in range(2):
                                v = nc.vector.tensor_tensor(y_place(b_lo, e, g, t), y_rows(e, heads),
                                                            y_place(b_hi, e, g, t).bitcast(F32), ALU.subtract)
                            v.then_inc(t_lo[0], 1)
                    for t, (qb, heads, h0, keys) in enumerate(TILES):
                        if p == S_AT[t]:
                            job = sm + g * 3 + (4 + t)
                            dve.wait_ge(small_done, job + 1)
                            dve.wait_ge(exp_done, tiles + g * 3 + (t + 1))
                            mask = mask0 if qb == 0 else mask1
                            sc = scores[:].rearrange("p (h k) -> p h k", h=heads)
                            nc.vector.scalar_tensor_tensor(
                                out=sc, in0=small.rearrange("p (h k) -> p h k", h=heads), scalar=DH**-0.5,
                                in1=mask[:].unsqueeze(1).broadcast_to([P, heads, keys]),
                                op0=ALU.mult, op1=ALU.add).then_inc(small_read, 1)
                            dve.wait_ge(small_read, job + 2)
                            soft0 = 4 * tiles + 12 * g + 4 * t
                            m = mx[:, 0:heads]
                            snk = sink[:, bass.ds(h0 + g * GQ + l * HQ, heads)]
                            nc.vector.tensor_reduce(m, sc, AX.X, ALU.max).then_inc(soft, 1)
                            dve.wait_ge(soft, soft0 + 1)
                            nc.vector.tensor_tensor(m, m, snk, ALU.max).then_inc(soft, 1)
                            dve.wait_ge(soft, soft0 + 2)
                            nc.vector.tensor_scalar(nmx[:, 0:heads], m, -1.0, None, ALU.mult).then_inc(soft, 1)
                            nc.vector.tensor_tensor(sd[:, 0:heads], snk, m, ALU.subtract).then_inc(soft, 1)

                with dve.Fori(0, NCH) as g:
                    ng = nl + U_G + g * (2 * UNITS)
                    for u in splitting(ng, 0, UNITS):
                        if u == 0:
                            with dve.If(g == 0):
                                evac_q(0, ng, bias0 + 3, cp + 6, 3 * l + 2, s0 + 3)
                            with dve.Else():
                                evac_proj(1, ng, bias1 + g + 2, lambda tb: gates[:, tb, bass.ds(D - N + g * N, N)],
                                          set_read[1])
                        attention(u, g)
                    for u in splitting(ng + UNITS, 0, UNITS):
                        if u == 0:
                            evac_proj(0, ng + UNITS, bias0 + g + 4, lambda tb: gates[:, tb, bass.ds(g * N, N)],
                                      set_read[0])
                        attention(UNITS + u, g)

                def gate_attn(s, used, c, sig):
                    dve.wait_ge(unit_used, used + SLOTS)
                    dve.wait_ge(sig_done, sig)
                    blk = gates[:, :, bass.ds(c * N, N)]
                    nc.vector.tensor_tensor(blk, acc[:, s], blk, ALU.mult).then_inc(set_read[s], 1)

                def merge(s, used, c, k):
                    dve.wait_ge(unit_used, used + SLOTS)
                    dve.wait_ge(t_done[1], j1 + T1["m"] + c)
                    dve.wait_ge(cp_done, cp + 8)
                    dve.wait_ge(sig_done, 8 * l + 8)
                    nc.vector.tensor_tensor(st[:], acc[:, s], gates[:, :, bass.ds(c * N + D, N)],
                                            ALU.mult).then_inc(set_read[s], 1)
                    dve.wait_ge(set_read[s], k + 2)
                    nc.vector.tensor_tensor(st[:], st[:], gates[:, :, bass.ds(c * N, N)], ALU.add).then_inc(st_ready, 1)

                hu = UNITS // 2
                with dve.Fori(0, 2) as i:
                    ni = nl + U_ATT + i * UNITS
                    for u in splitting(ni, 0, hu):
                        if u == 0:
                            with dve.If(i == 0):
                                evac_proj(1, ni, bias1 + (B_SET1 - 1), lambda tb: gates[:, tb, 2 * D - N:], set_read[1])
                            with dve.Else():
                                gate_attn(1, ni, 1, 8 * l + 4)
                    for u in splitting(ni + hu, 0, hu):
                        if u == 0:
                            gate_attn(0, ni + hu, 2 * i, 8 * l + 4 * i + 2)
                with dve.Fori(0, 2) as i:
                    ni = nl + U_SGU + i * UNITS
                    for u in splitting(ni, 0, hu):
                        if u == 0:
                            with dve.If(i == 0):
                                gate_attn(1, ni, 3, 8 * l + 8)
                            with dve.Else():
                                merge(1, ni, 1, s1 + SET1["sgu"])
                        if u == 2:
                            with dve.If(i == 1):
                                lo_pair(j0 + (T0["m"] + 1), j1 + (T1["m"] + 1), a_hi, a_lo, 4)
                    for u in splitting(ni + hu, 0, hu):
                        if u == 0:
                            merge(0, ni + hu, 2 * i, s0 + SET0["sgu"] + i)
                        if u == 2:
                            lo_pair(j0 + T0["m"] + 2 * i, j1 + T1["m"] + 2 * i, a_hi, a_lo, 8 * i)
                n2 = G_N2 + l * KB
                with dve.Fori(0, 2) as i:
                    ni = nl + U_WO + i * (2 * UNITS)
                    for u in splitting(ni, 0, UNITS):
                        if u == 0:
                            with dve.If(i == 0):
                                merge(1, ni, 3, s1 + (SET1["sgu"] + 1))
                            with dve.Else():
                                evac_residual(1, ni, 1, True, N_SAVE * l + 1, j1 + (T1["h"] + 1))
                        if u == 2:
                            with dve.If(i == 0):
                                lo_pair(j0 + (T0["m"] + 3), j1 + (T1["m"] + 3), a_hi, a_lo, KB - 4)
                            with dve.Else():
                                lo_pair(j0 + (T0["h"] + 1), j1 + (T1["h"] + 1), b_hi, b_lo, 4, n2 + 4)
                    for u in splitting(ni + UNITS, 0, UNITS):
                        if u == 0:
                            evac_residual(0, ni + UNITS, 2 * i, True, N_SAVE * l + 2 * i, j1 + T1["h"] + 2 * i)
                        if u == 2:
                            lo_pair(j0 + T0["h"] + 2 * i, j1 + T1["h"] + 2 * i, b_hi, b_lo, 8 * i, n2 + 8 * i)

                def swiglu(used, k_silu, j1_free, saved):
                    dve.wait_ge(unit_used, used + SLOTS)
                    dve.wait_ge(silu_done, k_silu)
                    dve.wait_ge(t_done[1], j1_free)
                    dve.wait_ge(h_saved, saved + 1)
                    for tb in range(TB):
                        v = nc.vector.scalar_tensor_tensor(out=st[:, tb], in0=acc[:, 1, tb], scalar=rs_h[:, tb:tb + 1],
                                                           in1=gst[:, tb], op0=ALU.mult, op1=ALU.mult)
                    v.then_inc(set_read[1], 1)

                def ffn_group(n0, m0, d0, n_j, units, last, group):
                    a0, a1 = j0 + T0["a"] + m0, j1 + T1["a"] + m0
                    silu0 = N_J * l + m0
                    saved = N_SAVE * l + 4
                    with dve.Fori(0, n_j) as j:
                        nj = n0 + j * (2 * UNITS)
                        for u in splitting(nj, 0, UNITS):
                            if u == 0:
                                if last:
                                    with dve.If(j == 0):
                                        evac_residual(1, nj, 3, False)
                                else:
                                    with dve.If(group * FJ + j == 0):
                                        evac_residual(1, nj, 3, True, N_SAVE * l + 3, j1 + (T1["h"] + 3))
                                    with dve.If(group * 2 * FJ + j == 2 * FJ):
                                        evac_residual(1, nj, 3, False)
                                with dve.If(j != 0):
                                    swiglu(nj, silu0 + j, a1 + j - 1, saved)
                            if u == 2:
                                if not last:
                                    with dve.If(group * FJ + j == 0):
                                        lo_pair(j0 + (T0["h"] + 3), j1 + (T1["h"] + 3), b_hi, b_lo, KB - 4,
                                                n2 + (KB - 4))
                                with dve.If(j != 0):
                                    lo_pair(a0 + j - 1, a1 + j - 1, c_hi, c_lo, not_negative(4 * j - 4))
                        for u in splitting(nj + UNITS, 0, UNITS):
                            if u == 0:
                                dve.wait_ge(unit_used, nj + (UNITS + SLOTS))
                                dve.wait_ge(rs_ready, 2 * l + 2)
                                for tb in range(TB):
                                    v = nc.vector.tensor_scalar(gst[:, tb], acc[:, 0, tb], rs_h[:, tb:tb + 1], None,
                                                                ALU.mult)
                                v.then_inc(set_read[0], 1)

                    def evac_down(s, used, c, saved, job):
                        if not last:
                            evac_residual(s, used, c, False)
                            return
                        with dve.If(l != DEPTH - 1):
                            evac_residual(s, used, c, True, saved, j1 + job)
                        with dve.Else():
                            evac_residual(s, used, c, True, saved, j1 + T1["x"])

                    with dve.Fori(0, 2) as i:
                        nd = n0 + n_j * 2 * UNITS + i * (2 * units)
                        for u in splitting(nd, 0, units):
                            if u == 0:
                                with dve.If(i == 0):
                                    swiglu(nd, silu0 + n_j, a1 + (n_j - 1), saved)
                                with dve.Else():
                                    evac_down(1, nd, 1, saved + 1, T1["x"] + 1)
                            if u == 2:
                                with dve.If(i == 0):
                                    lo_pair(a0 + (n_j - 1), a1 + (n_j - 1), c_hi, c_lo, 4 * (n_j - 1))
                                if last:
                                    with dve.If(l * 2 + i == 1):
                                        lo_pair(j0 + (T0["x"] + 1), j1 + (T1["x"] + 1), a_hi, a_lo, 4,
                                                (l + 1) * KB + 4)
                        for u in splitting(nd + units, units, units, stop=l * 2 + i if last else None):
                            if u == 0:
                                evac_down(0, nd + units, 2 * i, saved + 2 * i, 2 * i + T1["x"])
                            if u == 2 and last:
                                with dve.If(l != DEPTH - 1):
                                    lo_pair(j0 + T0["x"] + 2 * i, j1 + T1["x"] + 2 * i, a_hi, a_lo, 8 * i,
                                            (l + 1) * KB + 8 * i)

                with dve.Fori(0, FULL_GROUPS) as f:
                    ffn_group(nl + U_FF + f * GRP_UNITS, f * FJ, f * (FJ + 2), FJ, UNITS, False, f)
                ffn_group(nl + U_LAST, FULL_GROUPS * FJ, FULL_GROUPS * (FJ + 2), J_LAST, DOWN_LAST, True, None)
                with dve.If(l != DEPTH - 1):
                    evac_residual(1, nl + NU, 3, True, N_SAVE * l + 7, j1 + (T1["x"] + 3))
                with dve.Else():
                    dve.wait_ge(fin_landed, 16)
                    dve.wait_ge(h_saved, N_SAVE * DEPTH)
                    nc.vector.tensor_tensor(z[:, :, 0:D - N], h[:, :, 0:D - N],
                                            fin_g[:, 0:D - N].unsqueeze(1).broadcast_to([P, TB, D - N]),
                                            ALU.mult).then_inc(fin_step, 1)
                    evac_residual(1, nl + NU, 3, True, N_SAVE * l + 7, j1 + T1["x"])

            dve.wait_ge(set_read[1], DEPTH * N_SET1 + 1)
            nc.vector.tensor_tensor(z[:, :, D - N:], st[:], fin_g[:, D - N:].unsqueeze(1).broadcast_to([P, TB, N]),
                                    ALU.mult).then_inc(fin_step, 1)
            dve.wait_ge(fin_step, 2)
            dve.wait_ge(rs_ready, 2 * DEPTH + 1)
            for half in range(2):
                cols = slice(half * D // 2, (half + 1) * D // 2)
                nc.vector.tensor_scalar(z[:, 0, cols], z[:, 0, cols], rs_x[:, 0:1], None, ALU.mult).then_inc(fin_step, 1)


_INS = ["x", "positions", "norm1_g", "w_in", "b_in", "sinks", "sgu_ln_g", "sgu_ln_b", "sgu_w", "sgu_b",
        "w_attn_branch", "w_sgu_branch", "w_out", "norm2_g", "w_gate_up", "w_down", "final_g"]
_OUTS = [((1, SEQ, D), "float32")]


def kernel(**inputs):
    import numpy as _np
    import concourse.bacc as _bacc
    from concourse import mybir as _mybir
    from concourse.bass_utils import run_bass_kernel_spmd as _run

    nc = _bacc.Bacc("TRN2", target_bir_lowering=False, num_devices=1, dynamic_dma_scratch_size=1024)
    arrays, args = {}, []
    for name in _INS:
        a = _np.ascontiguousarray(inputs[name])
        arrays[f"in_{name}_dram"] = a
        args.append(nc.dram_tensor(f"in_{name}_dram", a.shape, _mybir.dt.from_np(a.dtype), kind="ExternalInput").ap())
    for i, (shape, dtype) in enumerate(_OUTS):
        dt = _mybir.dt.from_np(_np.dtype(dtype))
        args.append(nc.dram_tensor(f"out_{i}_dram", shape, dt, kind="ExternalOutput").ap())
    trunk(nc, *args)
    r = _run(nc, [arrays], core_ids=[0])
    got = tuple(r.results[0][f"out_{i}_dram"] for i in range(len(_OUTS)))
    return got[0]
```
